# Optimizing a Trainium2 kernel written in Bass

```python
import jax, jax.numpy as jnp
from jax import lax
import numpy as np

D_MODEL = 1024
BATCH = 1
SEQ = 1024
DEPTH = 1
DEC_BATCH = 8
DEC_SEQ = 4
PAST_LEN = 8192
PAGE_SIZE = 128

HGRN_KD = 128
HGRN_HEADS = D_MODEL // HGRN_KD
HGRN_VD = D_MODEL // HGRN_HEADS
HGRN_K = HGRN_HEADS * HGRN_KD
HGRN_V = HGRN_HEADS * HGRN_VD
CHUNK = 16
CONV_DIM = D_MODEL
CONV_WIDTH = 31
D_FF = -(-8 * D_MODEL // (3 * 256)) * 256
EPS = 1e-6
IN_SIZES = (HGRN_K, HGRN_K, HGRN_V, HGRN_V, CONV_DIM, CONV_DIM, D_MODEL, D_MODEL)
IN_COLS = sum(IN_SIZES)
IN_SPLITS = tuple(int(s) for s in np.cumsum(IN_SIZES)[:-1])

kernel_name = "hgrn2_conformer_gated_hybrid_step"

def rmsnorm(x, w):
    xf = x.astype(jnp.float32)
    y = xf * lax.rsqrt(jnp.mean(xf * xf, axis=-1, keepdims=True) + EPS)
    return (y * w.astype(jnp.float32)).astype(x.dtype)

def chunked_gated_recurrence(q, logf, k, v, s0):
    n, l, h, kd = q.shape
    vd = v.shape[-1]
    c = min(CHUNK, l)
    pad = (-l) % c
    if pad:
        pw = ((0, 0), (0, pad), (0, 0), (0, 0))
        q, logf, k, v = (jnp.pad(a, pw) for a in (q, logf, k, v))
    nc = (l + pad) // c

    def to_chunks(a):
        return a.reshape(n, nc, c, h, a.shape[-1]).transpose(1, 0, 3, 2, 4)

    qs, gs, ks, vs = (to_chunks(a) for a in (q, logf, k, v))
    mask = jnp.tril(jnp.ones((c, c), dtype=bool))[:, :, None]

    def step(s, inp):
        qc, gc, kc, vc = inp
        b = jnp.cumsum(gc, axis=2)
        o_inter = jnp.einsum('nhtk,nhkv->nhtv', qc * jnp.exp(b), s)
        diff = b[:, :, :, None, :] - b[:, :, None, :, :]
        decay = jnp.where(mask, jnp.exp(jnp.where(mask, diff, 0.0)), 0.0)
        att = jnp.einsum('nhtk,nhtsk,nhsk->nhts', qc, decay, kc)
        o_intra = jnp.einsum('nhts,nhsv->nhtv', att, vc)
        b_last = b[:, :, -1:, :]
        s_new = jnp.exp(b_last[:, :, 0, :])[..., None] * s + jnp.einsum(
            'nhsk,nhsv->nhkv', kc * jnp.exp(b_last - b), vc)
        return s_new, o_inter + o_intra

    s_fin, o = lax.scan(step, s0, (qs, gs, ks, vs))
    o = o.transpose(1, 0, 3, 2, 4).reshape(n, nc * c, h, vd)[:, :l]
    return o, s_fin

def hgrn2_branch(q_raw, f_raw, i_raw, og_raw, lb, norm_w, s0):
    n, l, _ = q_raw.shape
    q = jax.nn.silu(q_raw.astype(jnp.float32)).reshape(n, l, HGRN_HEADS, HGRN_KD)
    f = lb + (1.0 - lb) * jax.nn.sigmoid(f_raw.astype(jnp.float32))
    logf = jnp.log(f).reshape(n, l, HGRN_HEADS, HGRN_KD)
    k = (1.0 - f).reshape(n, l, HGRN_HEADS, HGRN_KD)
    v = i_raw.astype(jnp.float32).reshape(n, l, HGRN_HEADS, HGRN_VD)
    o, s_fin = chunked_gated_recurrence(q, logf, k, v, s0.astype(jnp.float32))
    o = o * lax.rsqrt(jnp.mean(o * o, axis=-1, keepdims=True) + EPS)
    o = o.reshape(n, l, HGRN_V) * norm_w.astype(jnp.float32) * jax.nn.silu(og_raw.astype(jnp.float32))
    return o.astype(q_raw.dtype), s_fin

def conformer_conv_branch(a, b, buf, dw_w, dw_b, ln_w, ln_b):
    u = a * jax.nn.sigmoid(b)
    ext = jnp.concatenate([buf.astype(u.dtype), u], axis=1)
    y = lax.conv_general_dilated(ext, dw_w[:, None, :].astype(u.dtype), (1,), 'VALID',
                                 dimension_numbers=('NWC', 'WIO', 'NWC'),
                                 feature_group_count=CONV_DIM) + dw_b
    yf = y.astype(jnp.float32)
    mu = jnp.mean(yf, axis=-1, keepdims=True)
    var = jnp.mean(jnp.square(yf - mu), axis=-1, keepdims=True)
    yf = (yf - mu) * lax.rsqrt(var + EPS) * ln_w.astype(jnp.float32) + ln_b.astype(jnp.float32)
    out = jax.nn.silu(yf).astype(a.dtype)
    return out, ext[:, -(CONV_WIDTH - 1):, :]

def decoder_layer(x, c, s0, buf, w_ada, b_ada, norm_mix_w, w_in, b_in, lb, hgrn_norm_w,
                  conv_dw_w, conv_dw_b, conv_ln_w, conv_ln_b, w_out, norm_ffn_w, w_ffn_in, w_ffn_out):
    mod = jax.nn.silu(c) @ w_ada + b_ada
    sh1, sc1, g1, sh2, sc2, g2 = (m[:, None, :] for m in jnp.split(mod, 6, axis=-1))
    h = rmsnorm(x, norm_mix_w) * (1.0 + sc1) + sh1
    z = h @ w_in + b_in
    q_raw, f_raw, i_raw, og_raw, glu_a, glu_b, gate_a, gate_b = jnp.split(z, IN_SPLITS, axis=-1)
    o_a, s_new = hgrn2_branch(q_raw, f_raw, i_raw, og_raw, lb, hgrn_norm_w, s0)
    o_b, buf_new = conformer_conv_branch(glu_a, glu_b, buf, conv_dw_w, conv_dw_b, conv_ln_w, conv_ln_b)
    merged = jnp.concatenate([jax.nn.sigmoid(gate_a) * o_a, jax.nn.sigmoid(gate_b) * o_b], axis=-1) @ w_out
    x = x + g1 * merged
    h2 = rmsnorm(x, norm_ffn_w) * (1.0 + sc2) + sh2
    gg, uu = jnp.split(h2 @ w_ffn_in, 2, axis=-1)
    x = x + g2 * ((jax.nn.silu(gg) * uu) @ w_ffn_out)
    return x, s_new, buf_new

def setup_inputs(seed: int = 0) -> dict:
    key = jax.random.key(seed)
    ks = jax.random.split(key, 24)
    f32 = jnp.float32
    nrm = lambda k, shape, s: jax.random.normal(k, shape, f32) * s
    d = D_MODEL
    return {
        "x_prompt": nrm(ks[0], (BATCH, SEQ, d), 1.0),
        "x_sample": nrm(ks[1], (DEC_BATCH, DEC_SEQ, d), 1.0),
        "state_hgrn": nrm(ks[2], (DEPTH, DEC_BATCH, HGRN_HEADS, HGRN_KD, HGRN_VD), 0.5),
        "state_conv": nrm(ks[3], (DEPTH, DEC_BATCH, CONV_WIDTH - 1, CONV_DIM), 0.5),
        "c_prompt": nrm(ks[4], (BATCH, d), 1.0),
        "c_sample": nrm(ks[5], (DEC_BATCH, d), 1.0),
        "w_ada": nrm(ks[6], (DEPTH, d, 6 * d), 0.5 * d ** -0.5),
        "b_ada": nrm(ks[7], (DEPTH, 6 * d), 0.02),
        "norm_mix_w": 1.0 + nrm(ks[8], (DEPTH, d), 0.02),
        "w_in": nrm(ks[9], (DEPTH, d, IN_COLS), d ** -0.5),
        "b_in": nrm(ks[10], (DEPTH, IN_COLS), 0.02),
        "lb_logits": nrm(ks[11], (DEPTH + 1, HGRN_K), 1.0),
        "hgrn_norm_w": 1.0 + nrm(ks[12], (DEPTH, HGRN_V), 0.02),
        "conv_dw_w": nrm(ks[13], (DEPTH, CONV_WIDTH, CONV_DIM), CONV_WIDTH ** -0.5),
        "conv_dw_b": nrm(ks[14], (DEPTH, CONV_DIM), 0.02),
        "conv_ln_w": 1.0 + nrm(ks[15], (DEPTH, CONV_DIM), 0.02),
        "conv_ln_b": nrm(ks[16], (DEPTH, CONV_DIM), 0.02),
        "w_out": nrm(ks[17], (DEPTH, HGRN_V + CONV_DIM, d), (HGRN_V + CONV_DIM) ** -0.5),
        "norm_ffn_w": 1.0 + nrm(ks[18], (DEPTH, d), 0.02),
        "w_ffn_in": nrm(ks[19], (DEPTH, d, 2 * D_FF), d ** -0.5),
        "w_ffn_out": nrm(ks[20], (DEPTH, D_FF, d), D_FF ** -0.5),
        "norm_final_w": 1.0 + nrm(ks[21], (d,), 0.02),
    }

def reference(x_prompt, x_sample, state_hgrn, state_conv, c_prompt, c_sample, w_ada, b_ada,
              norm_mix_w, w_in, b_in, lb_logits, hgrn_norm_w, conv_dw_w, conv_dw_b, conv_ln_w,
              conv_ln_b, w_out, norm_ffn_w, w_ffn_in, w_ffn_out, norm_final_w):
    lb_table = jnp.cumsum(jax.nn.softmax(lb_logits.astype(jnp.float32), axis=0), axis=0)
    n_p = x_prompt.shape[0]
    xp, xs = x_prompt, x_sample
    sp_list, bp_list, ss_list, bs_list = [], [], [], []
    for layer in range(DEPTH):
        lw = (w_ada[layer], b_ada[layer], norm_mix_w[layer], w_in[layer], b_in[layer], lb_table[layer],
              hgrn_norm_w[layer], conv_dw_w[layer], conv_dw_b[layer], conv_ln_w[layer], conv_ln_b[layer],
              w_out[layer], norm_ffn_w[layer], w_ffn_in[layer], w_ffn_out[layer])
        s0_p = jnp.zeros((n_p, HGRN_HEADS, HGRN_KD, HGRN_VD), jnp.float32)
        buf0_p = jnp.zeros((n_p, CONV_WIDTH - 1, CONV_DIM), xp.dtype)
        xp, sp, bp = decoder_layer(xp, c_prompt, s0_p, buf0_p, *lw)
        xs, ss, bs = decoder_layer(xs, c_sample, state_hgrn[layer], state_conv[layer], *lw)
        sp_list.append(sp.astype(state_hgrn.dtype))
        bp_list.append(bp.astype(state_conv.dtype))
        ss_list.append(ss.astype(state_hgrn.dtype))
        bs_list.append(bs.astype(state_conv.dtype))
    y_prompt = rmsnorm(xp, norm_final_w)
    y_sample = rmsnorm(xs, norm_final_w)
    new_state_hgrn_prompt = jnp.stack(sp_list, axis=0)
    new_state_conv_prompt = jnp.stack(bp_list, axis=0)
    new_state_hgrn_sample = jnp.stack(ss_list, axis=0)
    new_state_conv_sample = jnp.stack(bs_list, axis=0)
    return (y_prompt, y_sample, new_state_hgrn_prompt, new_state_conv_prompt,
            new_state_hgrn_sample, new_state_conv_sample)


_drawn_inputs = setup_inputs


def setup_inputs(seed=0):
    import zlib

    import numpy as np

    out = dict(_drawn_inputs(seed))
    spreads = {}
    factors = {'norm_mix_w': 2.902,
     'hgrn_norm_w': 8.0,
     'conv_dw_b': 8.0,
     'conv_ln_w': 8.0,
     'conv_ln_b': 8.0,
     'norm_ffn_w': 8.0,
     'norm_final_w': 2.747}
    for name, (base, spread) in spreads.items():
        noise = np.random.default_rng([zlib.crc32(name.encode()), seed]).standard_normal(out[name].shape)
        drawn = base * np.exp(spread * noise) if base else spread * noise
        out[name] = __import__('jax').numpy.asarray(drawn.astype(out[name].dtype))
    for name, factor in factors.items():
        out[name] = (out[name] * factor).astype(out[name].dtype)
    return out
```

```python
from contextlib import ExitStack

import concourse.bass as bass
from concourse import mybir

F32, F32R, I32 = mybir.dt.float32, mybir.dt.float32r, mybir.dt.int32
ACT = mybir.ActivationFunctionType
ALU = mybir.AluOpType
ds = bass.ds

P = 128
D = 1024
NJ = D // P
TP = 1024
NS, LS = 8, 4
TS = NS * LS
T = TP + TS
G, GW = 3, T // 3
NC = TP // P
LV = 7
HB = P // 2
TAPS = 31
HIST = TAPS - 1
UT = HIST + TP
US = HIST + LS
FF = 2816
NF = FF // P
NSEQ = 1 + NS
EPS = 1e-6

SQ, SF, SV, SOG, SA, SB, SGA, SGB = range(8)
ORDER = (SA, SB, SV, SQ, SF, SOG, SGA)
NT = len(ORDER)
SH1, SC1, G1, SH2, SC2, G2 = range(6)
NADA = 4

V_BIN, V_MIX, V_HN, V_DWB, V_LNW, V_LNB, V_FFN, V_FIN = 0, 64, 72, 80, 88, 96, 104, 112
NVA = 120
V_ADA, V_LB0, V_LB1 = NVA, NVA + 48, NVA + 56
NVB = 64
V_DW = NVA + NVB
NDW = TAPS * NJ
NVEC = V_DW + NDW

N_VT0, N_VT1, N_MISC, N_DG0, N_DG1, N_LV = range(6)
(N_SATT, N_KT0, N_KT1, N_KTS, N_KV0, N_KV1, N_O0, N_O1, N_OS, N_KVS0, N_SS, N_KVS1, N_R0, N_R1, N_R2) = range(12, 27)
NFILL = 27
SLOTS = 4
ADA_AT = {N_MISC: 0, N_SATT: 1, N_KTS: 2, N_OS: 3}
ADA_BACK = {N_SATT: 0, N_KTS: 1, N_OS: 2, N_SS: 3}
ADA_COL, BACK_COL = 384, 368
NREADY = LV + 3
R_START, R_LEVEL, R_VBLK, R_RMS = 1, 2, LV + 2, LV + 3
CONV_SLOT = 10

REC7 = NFILL * (NJ - 1)
LAST = ([("rec", n) for n in range(5)] + [("mu", n) for n in range(3)] + [("rec", n) for n in range(5, NFILL)]
        + [("lnss", 0)] + [("lnr", n) for n in range(3)])
LAST_AT = {step: n for n, step in enumerate(LAST)}
LAST_SLOTS = 5
R_X2 = REC7 + len(LAST)
R_Y = R_X2 + 4
R_Y_GRP = 1 + 1 + 2 * 3

ZT = NT * NJ
Z_OUT = ZT + NJ
B_FFN = Z_OUT + 2 * NJ
T_FFN = Z_OUT + NJ
B_GRP = 2 * NF + 3 * NJ
T_GRP = NF + NJ
OUT_K = (8, 8, NF - 16)
CHUNKS = tuple((c * P, min(P, GW - c * P)) for c in range((GW + P - 1) // P))

P0_C, P0_VEC, P0_X = 0, 1, 2
P0_HIST = P0_X + 2 * (NC + 1)
P0_ROWS = P0_HIST + 5
N0 = P0_ROWS + 3
P0_ADA = P0_ROWS - 1
XBUF = 4
ROW_PARTS = ((0, 512), (512, 512), (1024, TS))


class Idx:

    def __init__(self, n, i=None, per=0):
        assert per % 2 == 0
        self.n, self.i, self.per = n, i, per

    def __add__(self, m):
        return Idx(self.n + m, self.i, self.per)

    @property
    def v(self):
        return self.n if self.i is None else self.i * self.per + self.n

    @property
    def half(self):
        return self.n // 2 if self.i is None else self.i * (self.per // 2) + self.n // 2

    @property
    def par(self):
        return self.n % 2


def wait(eng, sem, value):
    if isinstance(value, int) and value <= 0:
        return
    eng.wait_ge(sem, value)


def fill_in_slot(s):
    if s == N_R0:
        return None
    n = s - (s > N_R0)
    return n if n < NFILL else None


def heads(eng, body, end):
    for h in range(2):
        body(Idx(h), Idx(NT * h), Idx(NFILL * (h - 1)), h >= 1)
        end()
    with eng.Fori(1, NJ // 2) as i:
        for h in range(2):
            body(Idx(h, i, 2), Idx(NT * h, i, 2 * NT), Idx(NFILL * (h - 1), i, 2 * NFILL), True)
            end()


def wait_apart(eng, met, sem, value):
    if isinstance(value, int):
        wait(eng, sem, value)
        return
    value = eng.to_reg(value)
    eng.wait_ge(*met)
    eng.wait_ge(sem, value)


class Steps:

    def __init__(self, eng, chain, met):
        self.eng, self.chain, self.n, self.last, self.met = eng, chain, 0, None, met

    def do(self, ins):
        ins.then_inc(self.chain, 1)
        self.n += 1
        self.last = (self.chain, self.n)

    def tell(self, ins, sem, value):
        ins.then_inc(sem, 1)
        self.last = (sem, value)

    def settle(self):
        if self.last:
            self.eng.wait_ge(*self.last)

    def settle_apart(self):
        if self.last:
            wait_apart(self.eng, self.met, *self.last)

    def restart(self):
        self.settle_apart()
        if self.n:
            self.eng.sem_clear(self.chain)
        self.n, self.last = 0, None


def program(nc, x_prompt, x_sample, state_hgrn, state_conv, c_prompt, c_sample, w_ada, b_ada, norm_mix_w, w_in, b_in,
            lb_logits, hgrn_norm_w, conv_dw_w, conv_dw_b, conv_ln_w, conv_ln_b, w_out, norm_ffn_w, w_ffn_in,
            w_ffn_out, norm_final_w, y_prompt, y_sample, st_prompt, cv_prompt, st_sample, cv_sample):
    ctx = ExitStack()

    win_v, wada_v, wout_v, wfi_v, wfo_v = (
        w[0].rearrange("(k p) n -> p k n", p=P) for w in (w_in, w_ada, w_out, w_ffn_in, w_ffn_out))
    merged = nc.dram_tensor("merged_scratch", (2 * NJ, P, T), F32, kind="Internal").ap()
    xt_dram = nc.dram_tensor("xt_scratch", (NJ, P, T), F32, kind="Internal").ap()
    hist_dram = nc.dram_tensor("hist_scratch", (NJ, P, NS * HIST), F32, kind="Internal").ap()

    def at(name, shape, dt, offset):
        return nc.alloc_sbuf_tensor_at(name, shape, dt, offset=offset)

    class Place:
        def __init__(self, start, end):
            self.p, self.end, self.where = start, end, {}

        def __call__(self, name, shape, dt=F32):
            n = 4
            for s in shape[1:]:
                n *= s
            self.where[name] = self.p
            t = at(name, shape, dt, self.p)
            self.p += (n + 31) // 32 * 32
            assert self.p <= self.end, (name, self.p, self.end)
            return t

    EIGHT = NJ * T * 4
    A1 = 16512
    A2, B1, C1, C2, WR = (A1 + n * EIGHT for n in range(1, 6))
    DD, END = WR + 6 * 4096, nc.sbuf_usable_end

    h_hi, h_lo = at("h_hi", [P, NJ, T], F32R, A1), at("h_lo", [P, NJ, T], F32R, A2)
    xt = at("xt", [P, NJ, T], F32, B1)
    yb = at("yb", [P, NJ, T], F32, B1)
    m_lo = [at("m_lo_a", [P, NJ, T], F32R, A1), at("m_lo_b", [P, NJ, T], F32R, A2)]
    m_hi = [at("m_hi_a", [P, NJ, T], F32R, C1), at("m_hi_b", [P, NJ, T], F32R, B1)]
    x2 = at("x2", [P, NJ, T], F32, C2)
    mraw = [at(f"mraw{i}", [P, T], F32, C2 + (NJ - 2 + i) * T * 4) for i in range(2)]
    h2_hi, h2_lo = at("h2_hi", [P, NJ, T], F32R, A1), at("h2_lo", [P, NJ, T], F32R, A2)
    act_hi, act_lo = at("act_hi", [P, NF, GW], F32R, B1), at("act_lo", [P, NF, GW], F32R, B1 + NF * GW * 4)
    h2buf = at("h2buf", [P, GW], F32, B1 + 2 * NF * GW * 4)
    w_raw = [at(f"w_raw{i}", [P, 8, P], F32, WR + i * 4096) for i in range(2)]
    w_hi = [at(f"w_hi{i}", [P, 8, P], F32R, WR + (2 + i) * 4096) for i in range(2)]
    w_lo = [at(f"w_lo{i}", [P, 8, P], F32R, WR + (4 + i) * 4096) for i in range(2)]

    d = Place(DD, END)
    ta, tb = d("ta", [P, T]), d("tb", [P, T])
    tab = (ta, tb)
    ysum = d("ysum", [P, T])
    vec = d("vec", [P, NVEC])
    mod = d("mod", [P, 6 * NJ, NSEQ])
    ct = d("ct", [P, NJ, NSEQ])
    ident, ones = d("ident", [P, P]), d("ones", [P, 1])
    am = d("am", [P, NJ, NSEQ])
    lbs = d("lbs", [P, 4, NJ])
    ms9, rs9 = d("ms9", [P, NC + 1]), d("rs9", [P, NC + 1])

    r = Place(C1, WR)
    att = r("att", [P, NC, P])
    vtok, ktok = r("vtok", [P, NC, P]), r("ktok", [P, NC, P])
    S, S0 = r("S", [P, NC, P]), r("S0", [P, NS, P])
    k, qd, f = (r(n, [P, T]) for n in ("k", "qd", "f"))
    sqs, k0s, k1s, q0s, q1s = (r(n, [P, TS]) for n in ("sqs", "k0s", "k1s", "q0s", "q1s"))
    assert r.p <= C2
    r.p = C2
    q, v = r("q", [P, T]), r("v", [P, T])
    tot = r("tot", [P, T // 2 + T // 4 + 2 * P])
    up, us = r("up", [P, UT]), r("us", [P, NS, US])
    O, gate, aw = r("O", [P, T]), r("gate", [P, T]), r("aw", [P, 8, P])
    tail = r("tail", [P, HIST + TS])
    att_s = r("att_s", [TS, TS])
    vtok_s, ktok_s = r("vtok_s", [TS, P]), r("ktok_s", [TS, P])
    urow = r("urow", [HIST + TS, P])
    smask, bmask = r("smask", [TS, 3, TS], I32), r("bmask", [TS, NS])
    masks = d("masks", [P, LV, HB], I32)
    arow = r("arow", [NSEQ, P])
    sqp = at("sqp", [P, TP], F32, r.where["vtok"])
    vblk = at("vblk", [TS, NS, P], F32, r.where["ktok"])
    murow = at("murow", [P, T], F32, r.where["up"])

    e = Place(C1, WR)
    ada_w = [e(f"ada_w{i}", [P, 8, 2 * P]) for i in range(2)]
    xrow = [e(f"xrow{i}", [P, D]) for i in range(XBUF)]
    hrow = e("hrow", [NS // 2 * HIST, 2, D])
    ht = e("ht", [P, NJ, NS * HIST])
    crow, csig = e("crow", [NSEQ, D]), e("csig", [NSEQ, D])
    vrow = e("vrow", [P, 4, P])
    xsq = e("xsq", [P, T])
    hbuf = (ta, tb, xsq)

    Z = [ctx.enter_context(nc.psum_tensor(f"Z{i}", [P, G, 512], F32)) for i in range(2)]
    R = [ctx.enter_context(nc.psum_tensor(f"R{i}", [P, 512], F32)) for i in range(2)]

    def sem(name):
        return ctx.enter_context(nc.semaphore(name))

    def two(name):
        return [sem(f"{name}{i}") for i in range(2)]

    w_loaded = two("w_loaded")
    w_hi_ready, w_split = sem("w_hi_ready"), sem("w_split")
    block_done = sem("block_done")
    z_free = two("z_free")
    fill_done, fill_evac = sem("fill_done"), sem("fill_evac")
    operands_ready, sig_ready, fk_ready = sem("operands_ready"), sem("sig_ready"), sem("fk_ready")
    gate_ready, u_ready, conv_done, ysum_ready = sem("gate_ready"), sem("u_ready"), sem("conv_done"), sem("ysum_ready")
    hist_loaded, square_ready, root_ready = sem("hist_loaded"), sem("square_ready"), sem("root_ready")
    s0_loaded, s0_stored, state_stored = sem("s0_loaded"), sem("s0_stored"), sem("state_stored")
    m_stored, u_stored, ada_loaded, masks_ready = sem("m_stored"), sem("u_stored"), sem("ada_loaded"), sem("masks_ready")
    const_ready = sem("const_ready")
    met = (const_ready, 2)
    vchain, gchain = sem("vchain"), sem("gchain")
    rows_loaded, c_loaded, hrow_loaded, hist_copied = (
        sem("rows_loaded"), sem("c_loaded"), sem("hrow_loaded"), sem("hist_copied"))
    x_loaded = [sem(f"x_loaded{i}") for i in range(XBUF)]
    adaw_loaded, adaw_used, adaw_read = two("adaw_loaded"), sem("adaw_used"), sem("adaw_read")
    csig_ready, c_ready, x_squared = (
        sem("csig_ready"), sem("c_ready"), sem("x_squared"))
    p0_done, p0_evac = sem("p0_done"), sem("p0_evac")
    ms_ready, rms_root, rms_ready = sem("ms_ready"), sem("rms_root"), sem("rms_ready")
    lb_in, lb_exp = sem("lb_in"), sem("lb_exp")
    h_full, h_hi_ready, h_ready = sem("h_full"), sem("h_hi_ready"), sem("h_ready")
    xt_stored, ht_stored = sem("xt_stored"), sem("ht_stored")
    centred, ln_squared, ln_added, ln_root, ln_recip = (
        sem("centred"), sem("ln_squared"), sem("ln_added"), sem("ln_root"), sem("ln_recip"))
    ln_scaled, ln_affine, ln_done = sem("ln_scaled"), sem("ln_affine"), sem("ln_done")
    gb_stored = two("gb_stored")
    m_loaded, m_prod, m_hi_ready, m_split = two("m_loaded"), sem("m_prod"), sem("m_hi_ready"), sem("m_split")
    xr_loaded, x2_squared, x2_summed = two("xr_loaded"), sem("x2_squared"), sem("x2_summed")
    x2_root, x2_recip = sem("x2_root"), sem("x2_recip")
    h2_full, h2_hi_ready, h2_ready = sem("h2_full"), sem("h2_hi_ready"), sem("h2_ready")
    g_sig, a_full, a_hi_ready, a_ready = sem("g_sig"), sem("a_full"), sem("a_hi_ready"), sem("a_ready")
    x3_squared, x3_summed, y_root, y_recip = sem("x3_squared"), sem("x3_summed"), sem("y_root"), sem("y_recip")
    y_stored = two("y_stored")

    def zfree(tile):
        return z_free[tile.par], tile.half + 1

    def loaded(b):
        return w_loaded[b.par], (b.half + 1) * 16

    def z3(par):
        return Z[par][:, :, 0:GW]

    def g3(ap):
        return ap.rearrange("p (g n) -> p g n", g=G)

    def at_head(tensor, h):
        return tensor[:, ds(h, 1), :].rearrange("p o t -> p (o t)")

    def column(base, h):
        return vec[:, ds(base + h, 1)]

    def seqs(ap):
        return ap.rearrange("p (s t) -> p s t", t=LS)

    def per_seq(ap):
        return ap.unsqueeze(2).to_broadcast([P, NS, LS])

    def lbcol(row, h):
        return lbs[:, row, ds(h, 1)]

    def halves(ap, b, which):
        return ap.rearrange("p (n two b) -> p n two b", two=2, b=b)[:, :, which, :]

    T_AT = (None, 0, T // 2, T // 2 + T // 4, T // 2 + T // 4 + 128, T // 2 + T // 4 + 192,
            T // 2 + T // 4 + 224, T // 2 + T // 4 + 240)

    def totals(l):
        n = (T, T // 2, T // 4, 128, 64, 32, 16, 8)[l]
        return f[:, 0:T] if l == 0 else tot[:, T_AT[l]:T_AT[l] + n]

    def p0_bank(n):
        return Z[n // 3 % 2][:, n % 3, :]

    def rec7(n):
        return Idx(REC7 + LAST_AT[("rec", n)])

    with ctx:
        block = ctx.enter_context(nc.Block())

        @block.sync
        def _(sp):
            def load_block(b, src, n=8):
                wait_apart(sp, met, w_split, b.v if b.i is None and b.n < 2 else (b + (-1)).v)
                sp.dma_start(w_raw[b.par][:, 0:n, :], src).then_inc(w_loaded[b.par], 16)

            sp.dma_start(crow[0:1, :], c_prompt).then_inc(c_loaded, 16)
            sp.dma_start(crow[1:NSEQ, :], c_sample).then_inc(c_loaded, 16)

            def load_x(t):
                if t >= XBUF:
                    sp.wait_ge(x_squared, t - XBUF + 1)
                    sp.wait_ge(p0_done, P0_X + 2 * (t - XBUF + 1))
                n = P if t < NC else TS
                src = x_prompt[0, t * P:(t + 1) * P, :] if t < NC else x_sample.rearrange("s t d -> (s t) d")
                sp.dma_start(xrow[t % XBUF][0:n, :], src).then_inc(x_loaded[t % XBUF], 16)

            def load_ada_cols(n):
                if n >= 2:
                    sp.wait_ge(adaw_used, n - 1)
                sp.dma_start(ada_w[n % 2][:, :, :], wada_v[:, :, n * 2 * P:(n + 1) * 2 * P]) \
                    .then_inc(adaw_loaded[n % 2], 16)

            load_x(0)
            load_x(1)

            def rows(row, tile, src):
                sp.dma_start(vrow[row:row + src.shape[0], tile, :], src).then_inc(rows_loaded, 16)

            for row, w in ((V_BIN, b_in), (V_MIX, norm_mix_w), (V_HN, hgrn_norm_w), (V_DWB, conv_dw_b),
                           (V_LNW, conv_ln_w), (V_LNB, conv_ln_b), (V_FFN, norm_ffn_w)):
                rows(row, 0, w[0].rearrange("(r c) -> r c", c=P))
            rows(V_FIN, 0, norm_final_w.rearrange("(r c) -> r c", c=P))
            rows(0, 1, b_ada[0].rearrange("(r c) -> r c", c=P))
            rows(V_LB0 - NVA, 1, lb_logits.rearrange("l (r c) -> (l r) c", c=P))
            taps = conv_dw_w[0].rearrange("t (r c) -> (t r) c", c=P)
            for n in range(2):
                rows(0, 2 + n, taps[n * NDW // 2:(n + 1) * NDW // 2, :])
            load_ada_cols(0)
            load_x(2)
            load_ada_cols(1)
            load_x(3)
            old = state_conv[0].rearrange("(two s) w d -> two (s w) d", two=2)
            for m in range(2):
                sp.dma_start(hrow[:, m, :], old[m]).then_inc(hrow_loaded, 16)
            for n in range(2, 8):
                load_ada_cols(n)
                if n + 2 <= NC:
                    load_x(n + 2)
            for b in range(2):
                load_block(Idx(b), win_v[:, :, ORDER[b] * D:ORDER[b] * D + P])
            sp.dma_start(cv_sample[0, :, 0:HIST - LS, :], state_conv[0, :, LS:HIST, :]).then_inc(hist_copied, 16)
            sp.wait_ge(p0_evac, P0_ROWS)
            sp.dma_start(hist_dram.rearrange("j p w -> p j w"), ht[:, :, :]).then_inc(ht_stored, 16)
            sp.dma_start(xt_dram.rearrange("j p t -> p j t"), xt[:, :, :]).then_inc(xt_stored, 16)
            sp.wait_ge(ht_stored, 16)
            sp.wait_ge(xt_stored, 16)
            sp.wait_ge(x_squared, NC + 1)
            sp.wait_ge(h_ready, NJ)
            sp.wait_ge(adaw_used, 8)

            def load_ada(hh, p):
                sp.dma_start(aw[:, :, :], wada_v[:, :, ds(hh.v * P + (G1 + p) * D, P)]).then_inc(ada_loaded, 16)

            def store_urow(hh, fill):
                wait_apart(sp, met, fill_evac, fill.v + 1)
                sp.dma_start(cv_prompt[0, 0, :, ds(hh.v * P, P)], urow[0:HIST, :]).then_inc(u_stored, 16)
                sp.dma_start(cv_sample[0, :, HIST - LS:HIST, ds(hh.v * P, P)], urow[HIST:HIST + TS, :]) \
                    .then_inc(u_stored, 16)

            def store_state(hh, fill):
                wait_apart(sp, met, fill_evac, fill.v + 1)
                sp.dma_start(st_prompt[0, 0, ds(hh.v, 1), :, :].rearrange("o k v -> (o k) v"), S[:, NC - 1, :]) \
                    .then_inc(state_stored, 16)

            def store_s0(hh, fill):
                sp.wait_ge(fill_evac, fill.v + 1)
                sp.dma_start(st_sample[0, :, ds(hh.v, 1), :, :].rearrange("s o k v -> k (s o) v"), S0[:, :, :]) \
                    .then_inc(s0_stored, 16)

            def load_s0(hh):
                wait(sp, s0_stored, hh.v * 16)
                sp.dma_start(S0[:, :, :], state_hgrn[0, :, ds(hh.v, 1), :, :].rearrange("s o k v -> k (s o) v")) \
                    .then_inc(s0_loaded, 16)

            def store_o(hh, fill):
                sp.wait_ge(fill_evac, fill.v + 1)
                sp.dma_start(merged[ds(hh.v, 1), :, :].rearrange("o p t -> (o p) t"), O[:, :]).then_inc(m_stored, 16)

            def ada_after(n, hh, fill):
                sp.wait_ge(fill_done, fill.v + 1)
                p = ADA_AT[n] + 1
                if p < NADA:
                    load_ada(hh, p)
                else:
                    load_ada(hh + 1, 0)

            def recurrence_io(j, hh, f, before, f_before):
                if before is not None:
                    if j == 0:
                        ada_after(N_OS, before, f_before + N_OS)
                    if j == 1:
                        store_s0(before, f_before + N_KVS1)
                        store_o(before, f_before + N_R2)
                if hh is not None:
                    if j == 2:
                        load_s0(hh)
                        store_urow(hh, f + N_MISC)
                        ada_after(N_MISC, hh, f + N_MISC)
                    if j == 5:
                        ada_after(N_SATT, hh, f + N_SATT)
                    if j == 6:
                        ada_after(N_KTS, hh, f + N_KTS)
                        store_state(hh, f + N_KV1)

            def body(h, t0, f, rec):
                for j in range(NT):
                    load_block(t0 + j, win_v[:, :, ds(h.v * P + ORDER[j] * D, P)]) if not (
                        h.i is None and h.n == 0 and j < 2) else None
                    if j == 1:
                        wait(sp, conv_done, h.v)
                        sp.dma_start(us[:, :, 0:HIST], hist_dram[ds(h.v, 1), :, :].rearrange(
                            "o p (s w) -> (o p) s w", w=HIST)).then_inc(hist_loaded, 16)
                        if not rec:
                            load_ada(h, 0)
                    early = h.i is None and h.n < 2
                    recurrence_io(j, h + (-1) if rec else None, f,
                                  None if early else h + (-2), None if early else f + (-NFILL))

            heads(sp, body, lambda: None)

            h7 = Idx(NJ - 1)
            for j in range(NJ):
                load_block(Idx(ZT + j), win_v[:, :, SGB * D + j * P:SGB * D + (j + 1) * P])
                recurrence_io(j, None, None, Idx(NJ - 2), Idx(REC7 - NFILL))
                if j == 2:
                    load_s0(h7)
                    store_urow(h7, rec7(N_MISC))
                    ada_after(N_MISC, h7, rec7(N_MISC))
                if j == 6:
                    ada_after(N_KTS, h7, rec7(N_KTS))
                if j >= 3:
                    sp.wait_ge(*zfree(Idx(ZT + j - 3)))
                    sp.dma_start(merged[NJ + j - 3], tab[(j - 3) % 2][:, :]).then_inc(gb_stored[(j - 3) % 2], 16)
                if j == 5:
                    ada_after(N_SATT, h7, rec7(N_SATT))
                if j == 7:
                    store_state(h7, rec7(N_KV1))
            for b in range(2):
                load_block(Idx(Z_OUT + b), wout_v[:, b * 8:b * 8 + 8, 0:P])
                j = NJ - 3 + b
                sp.wait_ge(*zfree(Idx(ZT + j)))
                sp.dma_start(merged[NJ + j], tab[j % 2][:, :]).then_inc(gb_stored[j % 2], 16)
            store_s0(h7, rec7(N_KVS1))
            store_o(h7, rec7(N_R2))
            j = NJ - 1
            sp.wait_ge(*zfree(Idx(ZT + j)))
            sp.dma_start(merged[NJ + j], tab[j % 2][:, :]).then_inc(gb_stored[j % 2], 16)

            sp.wait_ge(m_stored, 16 * NJ)
            sp.wait_ge(s0_stored, 16 * NJ)
            sp.wait_ge(state_stored, 16 * NJ)
            sp.wait_ge(u_stored, 32 * NJ)
            for i in range(2):
                sp.wait_ge(gb_stored[i], 16 * NJ // 2)

            def load_m(m):
                wait(sp, m_split, (m + (-1)).v)
                sp.dma_start(mraw[m.par][:, :], merged[ds(m.v, 1), :, :].rearrange("o p t -> (o p) t")) \
                    .then_inc(m_loaded[m.par], 16)

            def load_residual(j):
                wait(sp, x2_summed, (j + (-1)).v)
                sp.dma_start(tab[j.par][:, :], xt_dram[ds(j.v, 1), :, :].rearrange("o p t -> (o p) t")) \
                    .then_inc(xr_loaded[j.par], 16)

            def load_out_tile(ft):
                for kk in range(2):
                    load_block(Idx(Z_OUT + 2 * ft.n + kk, ft.i, 2 * ft.per),
                               wout_v[:, kk * 8:kk * 8 + 8, ds(ft.v * P, P)])

            for n in range(2):
                load_m(Idx(n))
            with sp.Fori(1, NJ // 2) as i:
                for n in range(2):
                    load_m(Idx(n, i, 2))
            load_out_tile(Idx(1))
            with sp.Fori(NJ // 2, NJ) as i:
                for n in range(2):
                    load_m(Idx(n, i, 2))
            for n in range(2):
                load_residual(Idx(n))
            load_out_tile(Idx(2))
            load_out_tile(Idx(3))
            with sp.Fori(1, NJ // 2 - 1) as i:
                for n in range(2):
                    load_residual(Idx(n, i, 2))
                for n in range(2):
                    load_out_tile(Idx(2 + n, i, 2))
            for n in range(2):
                load_residual(Idx(NJ - 2 + n))

            def ffn_in_block(g, f, kk):
                load_block(Idx(B_FFN + B_GRP * g + 2 * f.n + kk, f.i, 2 * f.per),
                           wfi_v[:, :, ds(f.v * P + kk * FF, P)])

            def store_y(g):
                for c, (c0, m) in enumerate(CHUNKS):
                    sp.wait_ge(fill_evac, R_Y + R_Y_GRP * g + 2 * c + 4)
                    t0 = g * GW + c0
                    src = tab[c % 2]
                    n = min(m, TP - t0)
                    sp.dma_start(y_prompt[0, t0:t0 + n, :], src[0:n, 0:D]).then_inc(y_stored[c % 2], 16)
                    if n < m:
                        sp.dma_start(y_sample.rearrange("s t d -> (s t) d"), src[n:m, 0:D]) \
                            .then_inc(y_stored[c % 2], 16)

            for g in range(G):
                for kk in range(2):
                    ffn_in_block(g, Idx(0), kk)
                if g:
                    store_y(g - 1)
                for kk in range(2):
                    ffn_in_block(g, Idx(1), kk)
                with sp.Fori(1, NF // 2) as i:
                    for n in range(2):
                        for kk in range(2):
                            ffn_in_block(g, Idx(n, i, 2), kk)
                with sp.Fori(0, NJ // 2) as i:
                    for n in range(2):
                        for kk in range(3):
                            load_block(Idx(B_FFN + B_GRP * g + 2 * NF + 3 * n + kk, i, 6),
                                       wfo_v[:, 8 * kk:8 * kk + OUT_K[kk], ds((i * 2 + n) * P, P)], OUT_K[kk])
            store_y(G - 1)
            sp.wait_ge(y_stored[0], 16 * (2 * G + 1))
            sp.wait_ge(y_stored[1], 16 * G)
            sp.wait_ge(hist_copied, 16)
            sp.wait_ge(s0_stored, 16 * NJ)
            sp.wait_ge(state_stored, 16 * NJ)
            sp.wait_ge(u_stored, 32 * NJ)

        @block.tensor
        def _(pe):
            mm, transpose = nc.tensor.matmul, nc.tensor.transpose

            pe.wait_ge(const_ready, 2)

            def fill0(n):
                if n >= 6:
                    pe.wait_ge(p0_evac, n - 5)
                return p0_bank(n)

            pe.wait_ge(c_ready, 1)
            bank = fill0(P0_C)
            for j in range(NJ):
                last = transpose(bank[:, j * NSEQ:(j + 1) * NSEQ], crow[:, j * P:(j + 1) * P], ident[0:NSEQ, 0:NSEQ])
            last.then_inc(p0_done, 1)
            pe.wait_ge(rows_loaded, 16 * 12)
            bank, col = fill0(P0_VEC), 0
            for tile, n in enumerate((NVA, NVB, NDW // 2, NDW // 2)):
                last = transpose(bank[:, col:col + n], vrow[0:n, tile, :], ident[0:n, 0:n])
                col += n
            last.then_inc(p0_done, 1)

            def ada_cols(n):
                pe.wait_ge(adaw_loaded[n % 2], 16 * (n // 2 + 1))
                if n >= 2:
                    pe.wait_ge(adaw_read, n - 1)
                for kt in range(NJ):
                    last = mm(R[n % 2][0:NSEQ, 0:2 * P], ct[:, kt, :], ada_w[n % 2][:, kt, :],
                              start=kt == 0, stop=kt == NJ - 1)
                last.then_inc(adaw_used, 1)

            pe.wait_ge(p0_evac, P0_C + 1)
            for t in range(NC + 1):
                pe.wait_ge(x_loaded[t % XBUF], 16 * (t // XBUF + 1))
                m = P if t < NC else TS
                for hf in range(2):
                    bank = fill0(P0_X + 2 * t + hf)
                    for j in range(4):
                        last = transpose(bank[:, j * m:(j + 1) * m],
                                         xrow[t % XBUF][0:m, (4 * hf + j) * P:(4 * hf + j + 1) * P], ident[0:m, 0:m])
                    last.then_inc(p0_done, 1)
                if t < 8:
                    ada_cols(t)
            pe.wait_ge(hrow_loaded, 32)
            m = NS // 2 * HIST
            for n in range(4):
                bank = fill0(P0_HIST + n)
                for j in range(2):
                    for row_tile in range(2):
                        c = (2 * j + row_tile) * m
                        last = transpose(bank[:, c:c + m], hrow[:, row_tile, (2 * n + j) * P:(2 * n + j + 1) * P],
                                         ident[0:m, 0:m])
                last.then_inc(p0_done, 1)
            bank = fill0(P0_ADA)
            pe.wait_ge(adaw_read, 8)
            for j in range(2 * NJ):
                last = transpose(bank[:, j * NSEQ:(j + 1) * NSEQ],
                                 tab[j // NJ][0:NSEQ, j % NJ * P:(j % NJ + 1) * P], ident[0:NSEQ, 0:NSEQ])
            last.then_inc(p0_done, 1)
            pe.wait_ge(rms_ready, 1)
            for n, (t0, w) in enumerate(ROW_PARTS):
                bank = fill0(P0_ROWS + n)
                for c in range(0, w, P):
                    m = min(P, w - c)
                    last = mm(bank[:, c:c + m], rs9[0:m, (t0 + c) // P:(t0 + c) // P + 1].to_broadcast([m, P]),
                              ident[0:m, 0:m], start=True, stop=True)
                last.then_inc(p0_done, 1)

            def products(b, outs, n, hi, lo, first, last_block, at_slot=None, slots=(), before_row=None):
                whi, wlo = w_hi[b.par], w_lo[b.par]
                pe.wait_ge(w_split, b.v + 1)
                for kt in range(n):
                    if before_row is not None:
                        before_row(kt)
                    for m, (w, x) in enumerate(((whi, hi), (whi, lo), (wlo, hi))):
                        for g, out in enumerate(outs):
                            last = mm(out, w[:, kt, :], x(kt, g), start=first and kt == 0 and m == 0,
                                      stop=last_block and kt == n - 1 and m == 2)
                    if kt == n - 1:
                        last.then_inc(block_done, 1)
                    for s in range(slots.count(kt)):
                        at_slot()

            def z_tile(b, at_slot=None, slots=(), before_row=None):
                t = b
                if t.i is None and t.n < 2:
                    pe.wait_ge(p0_evac, N0)
                else:
                    pe.wait_ge(*zfree(t + (-2)))
                products(b, [Z[t.par][:, g, 0:GW] for g in range(G)], NJ,
                         lambda kt, g: h_hi[:, kt, g * GW:(g + 1) * GW], lambda kt, g: h_lo[:, kt, g * GW:(g + 1) * GW],
                         True, True, at_slot, slots, before_row)

            def small(fill):
                if not (fill.i is None and fill.n < 2):
                    pe.wait_ge(fill_evac, (fill + (-1)).v)
                return R[fill.par]

            def tr(out, in_, m):
                return transpose(out, in_, ident[0:m, 0:m])

            def ada(bank, hh, p):
                pe.wait_ge(ada_loaded, (hh.v * NADA + (p + 1)) * 16)
                for kt in range(NJ):
                    last = mm(bank[0:NSEQ, ADA_COL:ADA_COL + P], ct[:, kt, :], aw[:, kt, :], start=kt == 0,
                              stop=kt == NJ - 1)
                return last

            def rows_of(bank, t0, w, recips):
                for c in range(0, w, P):
                    m = min(P, w - c)
                    i = (t0 + c) // P
                    last = mm(bank[:, c:c + m], recips[0:m, i:i + 1].to_broadcast([m, P]), ident[0:m, 0:m],
                              start=True, stop=True)
                return last

            def rec_fill(n, hh, fill, of):
                def ready(m):
                    pe.wait_ge(operands_ready, hh.v * NREADY + m)

                def read(m):
                    pe.wait_ge(fill_evac, of(m).v + 1)

                bank = small(fill)
                if n in (N_VT0, N_VT1):
                    if n == N_VT0:
                        pe.wait_ge(*zfree(Idx(NT * hh.n + ORDER.index(SV), hh.i, NT * hh.per)))
                    for c in range(4):
                        cc = c + 4 * (n - N_VT0)
                        last = tr(bank[:, c * P:(c + 1) * P], v[:, cc * P:(cc + 1) * P], P)
                elif n == N_MISC:
                    pe.wait_ge(u_ready, hh.v + 1)
                    tr(bank[0:TS, 0:P], v[:, TP:T], P)
                    last = tr(bank[0:HIST + TS, P:2 * P], tail[:, :], P)
                elif n in (N_DG0, N_DG1):
                    ready(R_START)
                    for c in range(4):
                        cc = (c + 4 * (n - N_DG0)) * P
                        last = mm(bank[:, c * P:(c + 1) * P], k[:, cc:cc + P], q[:, cc:cc + P], start=True, stop=True)
                elif N_LV <= n < N_LV + LV:
                    lv = n - N_LV
                    ready(R_START if lv == 0 else R_LEVEL + lv - 1)
                    for c in range(NC):
                        last = mm(bank[:, c * HB:(c + 1) * HB], k[:, c * P:(c + 1) * P],
                                  halves(qd[:, c * P:(c + 1) * P], 1 << lv, 1), start=True, stop=True)
                elif n == N_SATT:
                    ready(R_LEVEL + 1)
                    mm(bank[0:TS, 0:TS], k0s[:, :], q[:, TP:T], start=True, stop=True)
                    mm(bank[0:TS, TS:2 * TS], k0s[:, :], q0s[:, :], start=True, stop=True)
                    last = mm(bank[0:TS, 2 * TS:3 * TS], k1s[:, :], q1s[:, :], start=True, stop=True)
                elif n in (N_KT0, N_KT1):
                    ready(R_LEVEL + LV - 1)
                    for c in range(4):
                        cc = c + 4 * (n - N_KT0)
                        last = tr(bank[:, c * P:(c + 1) * P], k[:, cc * P:(cc + 1) * P], P)
                elif n == N_KTS:
                    last = tr(bank[0:TS, 0:P], k[:, TP:T], P)
                elif n in (N_KV0, N_KV1):
                    read(N_KT0 + n - N_KV0)
                    for c in range(4):
                        cc = c + 4 * (n - N_KV0)
                        last = mm(bank[:, c * P:(c + 1) * P], ktok[:, cc, :], vtok[:, cc, :], start=True, stop=True)
                elif n in (N_O0, N_O1):
                    read(N_KV0 + n - N_O0)
                    for c in range(4):
                        cc = c + 4 * (n - N_O0)
                        out = bank[:, c * P:(c + 1) * P]
                        last = mm(out, vtok[:, cc, :], att[:, cc, :], start=True, stop=cc == 0)
                        if cc:
                            last = mm(out, S[:, cc - 1, :], qd[:, cc * P:(cc + 1) * P], start=False, stop=True)
                elif n == N_OS:
                    pe.wait_ge(s0_loaded, (hh.v + 1) * 16)
                    mm(bank[:, 0:TS], vtok_s[:, :], att_s[:, :], start=True, stop=False)
                    for s in range(NS):
                        last = mm(bank[:, s * LS:(s + 1) * LS], S0[:, s, :], qd[:, TP + s * LS:TP + (s + 1) * LS],
                                  start=False, stop=s == NS - 1)
                elif n in (N_KVS0, N_KVS1):
                    hf = 0 if n == N_KVS0 else 1
                    ready(R_VBLK)
                    last = mm(bank[:, :], ktok_s[:, :], vblk[:, 4 * hf:4 * hf + 4, :], start=True, stop=True)
                elif n == N_SS:
                    pe.wait_ge(square_ready, hh.v + 1)
                    for c in range(NC):
                        mm(bank[:, c:c + 1], sqp[:, c * P:(c + 1) * P], ones[:, :], start=True, stop=True)
                    last = mm(bank[0:TS, NC:NC + 1], sqs[:, :], ones[:, :], start=True, stop=True)
                else:
                    if n == N_R0:
                        ready(R_RMS)
                    last = rows_of(bank, *ROW_PARTS[n - N_R0], rs9)
                if n in ADA_BACK:
                    last = tr(bank[:, BACK_COL:BACK_COL + NSEQ], arow[:, :], NSEQ)
                if n in ADA_AT:
                    last = ada(bank, hh, ADA_AT[n])
                last.then_inc(fill_done, 1)

            def token_sums(bank, row, n, lo=0):
                for c in range(0, n, P):
                    m = min(P, n - c)
                    last = mm(bank[0:m, c // P:c // P + 1], row[:, c:c + m], ones[:, :], start=True, stop=True)
                return last

            def body(h, t0, f, rec):
                at = [0]

                def slot():
                    n = fill_in_slot(at[0])
                    if rec and n is not None:
                        rec_fill(n, h + (-1), f + n, lambda m: f + m)
                    at[0] += 1

                for j in range(NT):
                    first = h.i is None and h.n == 0 and j == 0
                    z_tile(t0 + j, slot, (1, 3, 5, 7), (lambda kt: pe.wait_ge(h_ready, kt + 1)) if first else None)

            heads(pe, body, lambda: None)

            at = [0]

            def last_slot():
                n = at[0]
                at[0] += 1
                if n >= len(LAST):
                    return
                kind, m = LAST[n]
                fill = Idx(REC7 + n)
                if kind == "rec":
                    rec_fill(m, Idx(NJ - 1), fill, rec7)
                    return
                bank = small(fill)
                if kind == "mu":
                    if m == 0:
                        pe.wait_ge(ysum_ready, NJ)
                    t0, w = ROW_PARTS[m]
                    last = mm(bank[:, 0:w], ones[:, :].to_broadcast([P, P]), ysum[:, t0:t0 + w], start=True, stop=True)
                elif kind == "lnss":
                    pe.wait_ge(ln_added, NJ - 1)
                    last = token_sums(bank, ysum, T)
                else:
                    if m == 0:
                        pe.wait_ge(ln_recip, 1)
                    last = rows_of(bank, *ROW_PARTS[m], rs9)
                last.then_inc(fill_done, 1)

            for j in range(NJ):
                z_tile(Idx(ZT + j), last_slot, (1, 3, 5, 7, 7))

            def out_tile(ft):
                t = Idx(Z_OUT + ft.n, ft.i, ft.per)
                pe.wait_ge(*zfree(t + (-2)))
                for kk in range(2):
                    b = Idx(Z_OUT + 2 * ft.n + kk, ft.i, 2 * ft.per)
                    products(b, [Z[t.par][:, g, 0:GW] for g in range(G)], NJ,
                             lambda kt, g: m_hi[kk][:, kt, g * GW:(g + 1) * GW],
                             lambda kt, g: m_lo[kk][:, kt, g * GW:(g + 1) * GW], kk == 0, kk == 1,
                             before_row=lambda kt: pe.wait_ge(m_split, kk * NJ + kt + 1))

            with pe.Fori(0, NJ // 2) as i:
                for n in range(2):
                    out_tile(Idx(n, i, 2))

            fill = Idx(R_X2)
            bank = small(fill)
            pe.wait_ge(x2_summed, NJ)
            token_sums(bank, ysum, T).then_inc(fill_done, 1)
            for n, (t0, w) in enumerate(ROW_PARTS):
                bank = small(fill + (1 + n))
                if n == 0:
                    pe.wait_ge(x2_recip, 1)
                rows_of(bank, t0, w, rs9).then_inc(fill_done, 1)

            for g in range(G):
                cols = slice(g * GW, (g + 1) * GW)
                pe.wait_ge(h2_ready, NJ * (g + 1))
                with pe.Fori(0, NF // 2) as i:
                    for n in range(2):
                        t = Idx(T_FFN + T_GRP * g + n, i, 2)
                        pe.wait_ge(*zfree(t + (-2)))
                        for kk in range(2):
                            products(Idx(B_FFN + B_GRP * g + 2 * n + kk, i, 4), [Z[t.par][:, kk, 0:GW]], NJ,
                                     lambda kt, _: h2_hi[:, kt, cols], lambda kt, _: h2_lo[:, kt, cols], True, True)
                pe.wait_ge(a_ready, NF * (g + 1))
                with pe.Fori(0, NJ // 2) as i:
                    for n in range(2):
                        t = Idx(T_FFN + T_GRP * g + NF + n, i, 2)
                        pe.wait_ge(*zfree(t + (-2)))
                        for kk in range(3):
                            products(Idx(B_FFN + B_GRP * g + 2 * NF + 3 * n + kk, i, 6), [Z[t.par][:, 0, 0:GW]],
                                     OUT_K[kk], lambda kt, _: act_hi[:, 8 * kk + kt, :],
                                     lambda kt, _: act_lo[:, 8 * kk + kt, :], kk == 0, kk == 2)
                fill = Idx(R_Y + R_Y_GRP * g)
                bank = small(fill)
                pe.wait_ge(x3_summed, NJ * (g + 1))
                token_sums(bank, ysum, GW).then_inc(fill_done, 1)
                bank = small(fill + 1)
                pe.wait_ge(y_recip, g + 1)
                rows_of(bank, 0, GW, rs9).then_inc(fill_done, 1)
                for c, (c0, m) in enumerate(CHUNKS):
                    for hf in range(2):
                        bank = small(fill + (2 + 2 * c + hf))
                        if c == 0 and hf == 0:
                            pe.wait_ge(fill_evac, fill.v + 2)
                        for j in range(4):
                            last = tr(bank[0:m, j * P:(j + 1) * P],
                                      x2[:, 4 * hf + j, g * GW + c0:g * GW + c0 + m], P)
                        last.then_inc(fill_done, 1)

        @block.vector
        def _(dve):
            V = nc.vector
            st = Steps(dve, vchain, met)

            dve.wait_ge(c_loaded, 32)
            dve.wait_ge(csig_ready, 1)
            st.tell(V.tensor_tensor(crow[:, :], crow[:, :], csig[:, :], ALU.mult), c_ready, 1)

            def evac0(n, out, in_):
                dve.wait_ge(p0_done, n + 1)
                st.tell(V.tensor_copy(out, in_), p0_evac, n + 1)

            evac0(P0_C, ct[:, :, :], p0_bank(P0_C)[:, 0:NJ * NSEQ].rearrange("p (j s) -> p j s", s=NSEQ))
            evac0(P0_VEC, vec[:, :], p0_bank(P0_VEC)[:, 0:NVEC])
            l0, l1 = vec[:, V_LB0:V_LB0 + NJ], vec[:, V_LB1:V_LB1 + NJ]
            st.settle()
            st.do(V.tensor_tensor(lbs[:, 3, :], l0, l1, ALU.max))
            st.settle()
            st.do(V.tensor_tensor(lbs[:, 0, :], l0, lbs[:, 3, :], ALU.subtract))
            st.tell(V.tensor_tensor(lbs[:, 1, :], l1, lbs[:, 3, :], ALU.subtract), lb_in, 1)
            for t in range(NC + 1):
                m = P if t < NC else TS
                for hf in range(2):
                    n = P0_X + 2 * t + hf
                    evac0(n, xt[:, 4 * hf:4 * hf + 4, t * P:t * P + m],
                          p0_bank(n)[:, 0:4 * m].rearrange("p (j t) -> p j t", j=4))
                if t < 8:
                    dve.wait_ge(adaw_used, t + 1)
                    st.tell(V.tensor_copy(tab[t // 4][0:NSEQ, t % 4 * 2 * P:(t % 4 + 1) * 2 * P], R[t % 2][0:NSEQ, 0:2 * P]),
                            adaw_read, t + 1)
            dve.wait_ge(x_squared, NC + 1)
            st.do(V.tensor_scalar(ms9[:, 0:NC], ms9[:, 0:NC], 1.0 / D, EPS, ALU.mult, ALU.add))
            st.tell(V.tensor_scalar(ms9[0:TS, NC:NC + 1], ms9[0:TS, NC:NC + 1], 1.0 / D, EPS, ALU.mult, ALU.add),
                    ms_ready, 1)
            dve.wait_ge(lb_exp, 1)
            st.do(V.tensor_tensor(lbs[:, 3, :], lbs[:, 0, :], lbs[:, 1, :], ALU.add))
            st.settle()
            st.do(V.reciprocal(lbs[:, 3, :], lbs[:, 3, :]))
            st.settle()
            st.do(V.tensor_tensor(lbs[:, 0, :], lbs[:, 0, :], lbs[:, 3, :], ALU.mult))
            st.settle()
            st.do(V.tensor_scalar(lbs[:, 1, :], lbs[:, 0, :], -1.0, 1.0, ALU.mult, ALU.add))
            st.do(V.tensor_scalar(lbs[:, 2, :], lbs[:, 0, :], 1.0, None, ALU.subtract))
            dve.wait_ge(rms_root, 1)
            st.do(V.reciprocal(rs9[:, 0:NC], rs9[:, 0:NC]))
            st.tell(V.reciprocal(rs9[0:TS, NC:NC + 1], rs9[0:TS, NC:NC + 1]), rms_ready, 1)
            for n in range(4):
                evac0(P0_HIST + n, ht[:, 2 * n:2 * n + 2, :].rearrange("p j w -> p (j w)"),
                      p0_bank(P0_HIST + n)[:, 0:2 * NS * HIST])
            dve.wait_ge(p0_done, P0_ADA + 1)
            st.tell(V.tensor_tensor(mod[:, 0:2 * NJ, :],
                                    p0_bank(P0_ADA)[:, 0:2 * NJ * NSEQ].rearrange("p (j s) -> p j s", s=NSEQ),
                                    vec[:, V_ADA:V_ADA + 2 * NJ].unsqueeze(2).to_broadcast([P, 2 * NJ, NSEQ]),
                                    ALU.add), p0_evac, P0_ADA + 1)
            for n, (t0, w) in enumerate(ROW_PARTS):
                evac0(P0_ROWS + n, ysum[:, t0:t0 + w], p0_bank(P0_ROWS + n)[:, 0:w])
            def scales(sec, w):
                st.settle()
                st.do(V.tensor_scalar(am[:, :, :], mod[:, sec * NJ:(sec + 1) * NJ, :], 1.0, None, ALU.add))
                st.settle()
                st.do(V.tensor_tensor(am[:, :, :], am[:, :, :], vec[:, w:w + NJ].unsqueeze(2).to_broadcast(
                    [P, NJ, NSEQ]), ALU.mult))

            def modulate(out, x, row, j, shift, t0, t1, full, count):
                n = min(t1, TP) - t0
                ins = V.scalar_tensor_tensor(out[:, 0:n], x[:, 0:n], am[:, j, 0:1], row[:, 0:n], ALU.mult, ALU.mult)
                if t1 <= TP:
                    st.tell(ins, full, count)
                    return
                st.do(ins)
                s = seqs(out[:, n:n + TS])
                st.do(V.tensor_tensor(s, seqs(x[:, n:n + TS]), seqs(row[:, n:n + TS]), ALU.mult))
                st.settle()
                st.do(V.tensor_tensor(s, s, per_seq(am[:, j, 1:NSEQ]), ALU.mult))
                st.settle()
                st.tell(V.tensor_tensor(s, s, per_seq(mod[:, shift * NJ + j, 1:NSEQ]), ALU.add), full, count)

            scales(SC1, V_MIX)

            st.settle()
            for j in range(NJ):
                wait(dve, h_ready, j - 2)
                modulate(hbuf[j % 3][:, 0:T], xt[:, j, :], ysum[:, :], j, SH1, 0, T, h_full, j + 1)
            dve.wait_ge(h_ready, NJ)
            dve.wait_ge(xt_stored, 16)
            dve.wait_ge(ht_stored, 16)
            st.restart()

            def rec_start(hh):
                st.settle()
                st.do(V.tensor_tensor(qd[:, :], q[:, :], f[:, :], ALU.mult))
                st.do(V.tensor_copy(k0s[:, :], k[:, TP:T]))
                st.settle()
                st.tell(V.tensor_copy(q0s[:, :], qd[:, TP:T]), operands_ready, hh.v * NREADY + R_START)

            def rec_totals():
                for lv in range(1, LV + 1):
                    if lv > 1:
                        st.settle()
                    below = totals(lv - 1)[:, 0:2 * (TP >> lv) if lv > 2 else None]
                    n = (TP >> lv) + ((TS >> lv) if lv <= 2 else 0)
                    pairs = below[:, 0:2 * n].rearrange("p (n two) -> p n two", two=2)
                    st.do(V.tensor_tensor(totals(lv)[:, 0:n], pairs[:, :, 0], pairs[:, :, 1], ALU.mult))

            def level_up(lv, hh):
                b = 1 << lv
                n = T if lv <= 1 else TP
                pairs = totals(lv)[:, 0:n >> lv].rearrange("p (n two) -> p n two", two=2)
                shape = [P, n // (2 * b), b]
                late, early = halves(qd[:, 0:n], b, 1), halves(k[:, 0:n], b, 0)
                st.do(V.tensor_tensor(late, late, pairs[:, :, 0:1].to_broadcast(shape), ALU.mult))
                st.tell(V.tensor_tensor(early, early, pairs[:, :, 1:2].to_broadcast(shape), ALU.mult),
                        operands_ready, hh.v * NREADY + R_LEVEL + lv)
                if lv == 0:
                    st.settle()
                    st.do(V.tensor_copy(q1s[:, :], qd[:, TP:T]))
                    st.do(V.tensor_copy(k1s[:, :], k[:, TP:T]))
                    st.settle()

            def rec_evac(n, hh, fill):
                bank = R[fill.par]
                done = (fill_evac, fill.v + 1)

                def four(ap):
                    return ap.rearrange("p (c n) -> p c n", c=4)

                if n in (N_DG0, N_DG1):
                    wait_apart(dve, met, fill_done, fill.v + 1)
                else:
                    dve.wait_ge(fill_done, fill.v + 1)
                if n in ADA_BACK:
                    sec = (G1 + ADA_BACK[n]) * NJ
                    st.do(V.tensor_scalar(mod[:, ds(sec + hh.v, 1), :].rearrange("p o s -> p (o s)"),
                                          bank[:, BACK_COL:BACK_COL + NSEQ], column(V_ADA + sec, hh.v), None, ALU.add))
                if n in ADA_AT:
                    st.do(V.tensor_copy(arow[:, :], bank[0:NSEQ, ADA_COL:ADA_COL + P]))
                if n in (N_VT0, N_VT1):
                    st.tell(V.tensor_copy(vtok[:, 4 * n:4 * n + 4, :], four(bank[:, :])), *done)
                    if n == N_VT0:
                        rec_start(hh)
                elif n == N_MISC:
                    if not (hh.i is None and hh.n == 0):
                        wait(dve, u_stored, hh.v * 32)
                    st.do(V.tensor_copy(vtok_s[:, :], bank[0:TS, 0:P]))
                    st.tell(V.tensor_copy(urow[:, :], bank[0:HIST + TS, P:2 * P]), *done)
                    rec_totals()
                elif n in (N_DG0, N_DG1):
                    c = 4 * (n - N_DG0)
                    st.settle_apart()
                    st.tell(V.copy_predicated(att[:, c:c + 4, :], ident[:, :].bitcast(I32).unsqueeze(1).to_broadcast([P, 4, P]),
                                              four(bank[:, :])), *done)
                elif N_LV <= n < N_LV + LV:
                    lv = n - N_LV
                    b = 1 << lv
                    level_up(lv, hh)
                    out = att[:, :, :].rearrange("p c (n two b) -> p c n two b", two=2, b=b)[:, :, :, 1, :]
                    data = bank[:, :].rearrange("p (c n b) -> p c n b", c=NC, b=b)
                    mask = masks[:, lv, :].rearrange("p (n b) -> p n b", b=b).unsqueeze(1).to_broadcast(
                        [P, NC, HB // b, b])
                    st.settle_apart()
                    st.tell(V.copy_predicated(out, mask, data), *done)
                elif n == N_SATT:
                    for m in range(3):
                        st.settle_apart()
                        ins = V.copy_predicated(att_s[:, :], smask[:, m, :], bank[0:TS, m * TS:(m + 1) * TS])
                        st.do(ins) if m < 2 else st.tell(ins, *done)
                elif n in (N_KT0, N_KT1):
                    c = 4 * (n - N_KT0)
                    st.tell(V.tensor_copy(ktok[:, c:c + 4, :], four(bank[:, :])), *done)
                elif n == N_KTS:
                    st.tell(V.tensor_copy(ktok_s[:, :], bank[0:TS, 0:P]), *done)
                elif n in (N_KV0, N_KV1):
                    if n == N_KV1:
                        wait(dve, state_stored, hh.v * 16)
                    for c in range(4):
                        cc = c + 4 * (n - N_KV0)
                        add = bank[:, c * P:(c + 1) * P]
                        if cc == 0:
                            st.do(V.tensor_copy(S[:, 0, :], add))
                            continue
                        st.settle()
                        ins = V.scalar_tensor_tensor(S[:, cc, :], S[:, cc - 1, :], totals(LV)[:, cc:cc + 1], add,
                                                     ALU.mult, ALU.add)
                        st.do(ins) if c < 3 else st.tell(ins, *done)
                    if n == N_KV1:
                        st.tell(V.tensor_tensor(vblk[:, :, :], vtok_s[:, :].unsqueeze(1).to_broadcast([TS, NS, P]),
                                                bmask[:, :].unsqueeze(2).to_broadcast([TS, NS, P]), ALU.mult),
                                operands_ready, hh.v * NREADY + R_VBLK)
                elif n in (N_O0, N_O1):
                    if n == N_O0:
                        wait(dve, m_stored, hh.v * 16)
                    c = 4 * P * (n - N_O0)
                    st.tell(V.tensor_copy(O[:, c:c + 4 * P], bank[:, :]), *done)
                elif n == N_OS:
                    st.tell(V.tensor_copy(O[:, TP:T], bank[:, 0:TS]), *done)
                elif n in (N_KVS0, N_KVS1):
                    for s in range(4):
                        seq = s + (0 if n == N_KVS0 else 4)
                        ins = V.scalar_tensor_tensor(S0[:, seq, :], S0[:, seq, :],
                                                     totals(2)[:, TP // 4 + seq:TP // 4 + seq + 1],
                                                     bank[:, s * P:(s + 1) * P], ALU.mult, ALU.add)
                        st.do(ins) if s < 3 else st.tell(ins, *done)
                    if n == N_KVS1:
                        dve.wait_ge(root_ready, hh.v + 1)
                        st.do(V.reciprocal(rs9[:, 0:NC], rs9[:, 0:NC]))
                        st.tell(V.reciprocal(rs9[0:TS, NC:NC + 1], rs9[0:TS, NC:NC + 1]), operands_ready,
                                hh.v * NREADY + R_RMS)
                elif n == N_SS:
                    st.do(V.tensor_scalar(ms9[:, 0:NC], bank[:, 0:NC], 1.0 / P, EPS, ALU.mult, ALU.add))
                    st.tell(V.tensor_scalar(ms9[0:TS, NC:NC + 1], bank[0:TS, NC:NC + 1], 1.0 / P, EPS, ALU.mult,
                                            ALU.add), *done)
                    dve.wait_ge(gate_ready, hh.v + 1)
                    st.do(V.scalar_tensor_tensor(O[:, :], O[:, :], column(V_HN, hh.v), gate[:, :], ALU.mult, ALU.mult))
                else:
                    t0, w = ROW_PARTS[n - N_R0]
                    st.settle()
                    st.tell(V.tensor_tensor(O[:, t0:t0 + w], O[:, t0:t0 + w], bank[:, 0:w], ALU.mult), *done)

            def conv_tap(n, h):
                y = yb[:, ds(h.v, 1), :].rearrange("p o t -> p (o t)")
                w = column(V_DW + n * NJ, h.v)
                yp, ys = y[:, 0:TP], seqs(y[:, TP:T])
                xp, xs = up[:, n:n + TP], us[:, :, n:n + LS]
                if n == 0:
                    dve.wait_ge(u_ready, h.v + 1)
                    dve.wait_ge(hist_loaded, (h.v + 1) * 16)
                    bias = column(V_DWB, h.v)
                    st.do(V.tensor_scalar(yp, xp, w, bias, ALU.mult, ALU.add))
                    st.do(V.tensor_scalar(ys, xs, w, bias, ALU.mult, ALU.add))
                    return
                st.settle()
                st.do(V.scalar_tensor_tensor(yp, xp, w, yp, ALU.mult, ALU.add))
                ins = V.scalar_tensor_tensor(ys, xs, w, ys, ALU.mult, ALU.add)
                if n < TAPS - 1:
                    st.do(ins)
                else:
                    st.tell(ins, conv_done, h.v + 1)

            def tile_read(j, h, t0):
                t = t0 + j
                kind = ORDER[j]
                if kind in (SQ, SOG):
                    dve.wait_ge(sig_ready, h.v * 2 + (1 if kind == SQ else 2))
                    out = q if kind == SQ else tb
                    st.tell(V.scalar_tensor_tensor(g3(out[:, :]), z3(t.par), column(V_BIN + kind * NJ, h.v),
                                                   g3(tb[:, :]), ALU.add, ALU.mult), *zfree(t))
                elif kind == SF:
                    dve.wait_ge(*zfree(t))
                    st.do(V.tensor_scalar(f[:, :], ta[:, :], lbcol(1, h.v), lbcol(0, h.v), ALU.mult, ALU.add))
                    st.tell(V.tensor_scalar(k[:, :], ta[:, :], lbcol(2, h.v), lbcol(1, h.v), ALU.mult, ALU.add),
                            fk_ready, h.v + 1)

            def body(h, t0, fl, rec):
                taps = iter(range(TAPS))
                hh = h + (-1)
                for j in range(NT):
                    if j:
                        tile_read(j - 1, h, t0)
                    for s in range(SLOTS):
                        slot = SLOTS * j + s
                        n = fill_in_slot(slot)
                        if n == 0 and rec and h.i is None:
                            dve.wait_ge(masks_ready, 1)
                        if rec and n is not None:
                            rec_evac(n, hh, fl + n)
                        if slot >= CONV_SLOT and n not in (N_OS, N_SS):
                            for tap in (next(taps, None), next(taps, None)):
                                if tap is not None:
                                    conv_tap(tap, h)

            heads(dve, body, st.restart)

            h7 = Idx(NJ - 1)
            for n, (kind, m) in enumerate(LAST):
                fill = Idx(REC7 + n)
                bank = R[fill.par]
                if kind == "rec":
                    rec_evac(m, h7, fill)
                    continue
                dve.wait_ge(fill_done, fill.n + 1)
                if kind == "mu":
                    t0, w = ROW_PARTS[m]
                    st.tell(V.tensor_scalar(murow[:, t0:t0 + w], bank[:, 0:w], 1.0 / D, None, ALU.mult),
                            fill_evac, fill.n + 1)
                elif kind == "lnss":
                    st.do(V.tensor_scalar(ms9[:, 0:NC], bank[:, 0:NC], 1.0 / D, EPS, ALU.mult, ALU.add))
                    st.tell(V.tensor_scalar(ms9[0:TS, NC:NC + 1], bank[0:TS, NC:NC + 1], 1.0 / D, EPS, ALU.mult,
                                            ALU.add), fill_evac, fill.n + 1)
                    dve.wait_ge(ln_root, 1)
                    st.do(V.reciprocal(rs9[:, 0:NC], rs9[:, 0:NC]))
                    st.tell(V.reciprocal(rs9[0:TS, NC:NC + 1], rs9[0:TS, NC:NC + 1]), ln_recip, 1)
                else:
                    t0, w = ROW_PARTS[m]
                    st.tell(V.tensor_copy(ysum[:, t0:t0 + w], bank[:, 0:w]), fill_evac, fill.n + 1)
            st.settle()
            for j in range(NJ):
                dve.wait_ge(centred, j + 1)
                st.tell(V.tensor_tensor(yb[:, j, :], yb[:, j, :], ysum[:, :], ALU.mult), ln_scaled, j + 1)

            st.settle()
            st.do(V.memset(ysum[:, :], 0.0))
            st.restart()

            def m_low(m, which):
                dve.wait_ge(m_hi_ready, m.v + 1)
                st.tell(V.tensor_tensor(at_head(m_lo[which], m.v - which * NJ), mraw[m.par][:, :],
                                        at_head(m_hi[which], m.v - which * NJ).bitcast(F32), ALU.subtract),
                        m_split, m.v + 1)

            for which in range(2):
                with dve.Fori(which * NJ // 2, (which + 1) * NJ // 2) as i:
                    for n in range(2):
                        m_low(Idx(n, i, 2), which)
                    st.restart()

            def gated_add(out, base, psum, sec, j, t0, t1):
                n = min(t1, TP) - t0
                row = mod[:, ds(sec * NJ + j, 1), :].rearrange("p o s -> p (o s)")
                prompt = (out[:, 0:n], psum[:, 0:n], row[:, 0:1], base[:, 0:n], ALU.mult, ALU.add)
                if t1 <= TP:
                    return [lambda: V.scalar_tensor_tensor(*prompt)]
                so, sb, s = seqs(out[:, n:n + TS]), seqs(base[:, n:n + TS]), seqs(psum[:, n:n + TS])
                tmp = seqs(rowtmp[:, 0:TS])
                return [lambda: V.scalar_tensor_tensor(*prompt),
                        lambda: V.tensor_tensor(tmp, s, per_seq(row[:, 1:NSEQ]), ALU.mult),
                        lambda: V.tensor_tensor(so, sb, tmp, ALU.add)]

            rowtmp = masks[:, 0, :].bitcast(F32)

            def out_tile(ft):
                t = Idx(Z_OUT + ft.n, ft.i, ft.per)
                dve.wait_ge(block_done, (Idx(Z_OUT + 2 * ft.n + 1, ft.i, 2 * ft.per)).v + 1)
                dve.wait_ge(xr_loaded[ft.par], (ft.half + 1) * 16)
                res, out = tab[ft.par], at_head(x2, ft.v)
                todo = []
                for g in range(G):
                    a, b = g * GW, (g + 1) * GW
                    todo += gated_add(out[:, a:b], res[:, a:b], Z[t.par][:, g, 0:GW], G1, ft.v, a, b)
                for m, make in enumerate(todo):
                    if m == len(todo) - 1:
                        st.settle()
                        st.tell(make(), *zfree(t))
                    else:
                        st.do(make())
                dve.wait_ge(x2_squared, ft.v + 1)
                st.tell(V.tensor_tensor(ysum[:, :], ysum[:, :], res[:, :], ALU.add), x2_summed, ft.v + 1)

            with dve.Fori(0, NJ // 2) as i:
                for n in range(2):
                    out_tile(Idx(n, i, 2))
                st.restart()

            def mean_squares(bank, parts, div, fill):
                dve.wait_ge(fill_done, fill + 1)
                for n, (m, cols) in enumerate(parts):
                    ins = V.tensor_scalar(ms9[0:m, cols], bank[0:m, cols], 1.0 / div, EPS, ALU.mult, ALU.add)
                    st.do(ins) if n < len(parts) - 1 else st.tell(ins, fill_evac, fill + 1)

            def low(b, n=8):
                dve.wait_ge(w_hi_ready, b.v + 1)
                st.tell(V.tensor_tensor(w_lo[b.par][:, 0:n, :], w_raw[b.par][:, 0:n, :],
                                        w_hi[b.par][:, 0:n, :].bitcast(F32), ALU.subtract), w_split, b.v + 1)

            dve.wait_ge(w_split, B_FFN)
            low(Idx(B_FFN))
            low(Idx(B_FFN + 1))
            mean_squares(R[R_X2 % 2], ((P, slice(0, NC)), (TS, slice(NC, NC + 1))), D, R_X2)
            scales(SC2, V_FFN)
            dve.wait_ge(x2_root, 1)
            st.do(V.reciprocal(rs9[:, 0:NC], rs9[:, 0:NC]))
            st.tell(V.reciprocal(rs9[0:TS, NC:NC + 1], rs9[0:TS, NC:NC + 1]), x2_recip, 1)
            for n, (t0, w) in enumerate(ROW_PARTS):
                fill = R_X2 + 1 + n
                dve.wait_ge(fill_done, fill + 1)
                st.tell(V.tensor_copy(ysum[:, t0:t0 + w], R[fill % 2][:, 0:w]), fill_evac, fill + 1)

            st.settle()
            for j in range(NJ):
                wait(dve, h2_ready, j - 1)
                modulate(tab[j % 2][:, 0:GW], x2[:, j, 0:GW], ysum[:, 0:GW], j, SH2, 0, GW, h2_full, j + 1)

            for g in range(G):
                if g == 0:
                    dve.wait_ge(h2_ready, NJ)
                st.settle()
                st.do(V.memset(ysum[:, 0:GW], 0.0))
                st.restart()
                with dve.Fori(0, NF // 2) as i:
                    for n in range(2):
                        t = Idx(T_FFN + T_GRP * g + n, i, 2)
                        b = Idx(B_FFN + B_GRP * g + 2 * n, i, 4)
                        fi = Idx(n, i, 2)
                        count = fi.v + NF * g + 1
                        sg, a = ta[:, n * GW:(n + 1) * GW], tb[:, n * GW:(n + 1) * GW]
                        low(b + 2)
                        dve.wait_ge(g_sig, count)
                        st.do(V.tensor_tensor(sg, sg, Z[t.par][:, 0, 0:GW], ALU.mult))
                        dve.wait_ge(block_done, (b + 2).v)
                        st.settle()
                        st.tell(V.tensor_tensor(a, sg, Z[t.par][:, 1, 0:GW], ALU.mult), *zfree(t))
                        low(b + 3)
                        dve.wait_ge(a_hi_ready, count)
                        st.tell(V.tensor_tensor(act_lo[:, ds(fi.v, 1), :].rearrange("p o t -> p (o t)"), a,
                                                act_hi[:, ds(fi.v, 1), :].rearrange("p o t -> p (o t)").bitcast(F32),
                                                ALU.subtract), a_ready, count)
                    st.restart()

                def ffn_out(n, i, last_pass):
                    j = Idx(n, i, 2) if i is not None else Idx(n)
                    base = B_FFN + B_GRP * g + 2 * NF
                    b = Idx(base + 3 * n, i, 6) if i is not None else Idx(base + 3 * n)
                    t = Idx(T_FFN + T_GRP * g + NF + n, i, 2) if i is not None else Idx(T_FFN + T_GRP * g + NF + n)
                    for kk in range(3):
                        if not (last_pass and 3 * n + kk + 2 >= 3 * NJ):
                            low(b + (kk + 2), OUT_K[(kk + 2) % 3])
                    dve.wait_ge(block_done, (b + 2).v + 1)
                    a, e = g * GW, (g + 1) * GW
                    x = x2[:, ds(j.v, 1), a:e].rearrange("p o t -> p (o t)")
                    todo = gated_add(x, x, Z[t.par][:, 0, 0:GW], G2, j.v, a, e)
                    for m, make in enumerate(todo):
                        if m == len(todo) - 1:
                            st.settle()
                            st.tell(make(), *zfree(t))
                        else:
                            st.do(make())
                    count = j.v + NJ * g + 1
                    dve.wait_ge(x3_squared, count)
                    st.tell(V.tensor_tensor(ysum[:, 0:GW], ysum[:, 0:GW], tb[:, n % 2 * GW:(n % 2 + 1) * GW], ALU.add),
                            x3_summed, count)

                if g < G - 1:
                    with dve.Fori(0, NJ // 2) as i:
                        for n in range(2):
                            ffn_out(n, i, False)
                        st.restart()
                else:
                    with dve.Fori(0, NJ // 2 - 1) as i:
                        for n in range(2):
                            ffn_out(n, i, False)
                        st.restart()
                    for n in range(NJ - 2, NJ):
                        ffn_out(n, None, True)

                fill = R_Y + R_Y_GRP * g
                mean_squares(R[fill % 2], ((P, slice(0, 2)), (GW - 2 * P, slice(2, 3))), D, fill)
                dve.wait_ge(y_root, g + 1)
                st.do(V.reciprocal(rs9[:, 0:2], rs9[:, 0:2]))
                st.tell(V.reciprocal(rs9[0:GW - 2 * P, 2:3], rs9[0:GW - 2 * P, 2:3]), y_recip, g + 1)
                dve.wait_ge(fill_done, fill + 2)
                for j in range(NJ):
                    x = x2[:, j, g * GW:(g + 1) * GW]
                    ins = V.scalar_tensor_tensor(x, x, vec[:, V_FIN + j:V_FIN + j + 1], R[(fill + 1) % 2][:, 0:GW],
                                                 ALU.mult, ALU.mult)
                    st.do(ins) if j < NJ - 1 else st.tell(ins, fill_evac, fill + 2)
                for c, (c0, m) in enumerate(CHUNKS):
                    wait(dve, y_stored[c % 2], 16 * (g if c == 1 else 2 * g + c // 2))
                    for hf in range(2):
                        n = fill + 2 + 2 * c + hf
                        dve.wait_ge(fill_done, n + 1)
                        ins = V.tensor_copy(tab[c % 2][0:m, hf * 512:(hf + 1) * 512], R[n % 2][0:m, :])
                        st.tell(ins, fill_evac, n + 1)

        @block.scalar
        def _(act):
            A = nc.scalar.activation

            def hi(b, n=8):
                act.wait_ge(*loaded(b))
                if not (b.i is None and b.n < 2):
                    act.wait_ge(block_done, (b + (-1)).v)
                A(w_hi[b.par][:, 0:n, :], w_raw[b.par][:, 0:n, :], ACT.Copy).then_inc(w_hi_ready, 1)

            def root(parts, ready):
                for n, (m, cols) in enumerate(parts):
                    last = A(rs9[0:m, cols], ms9[0:m, cols], ACT.Sqrt)
                last.then_inc(ready, 1)

            NINE = ((P, slice(0, NC)), (TS, slice(NC, NC + 1)))

            act.wait_ge(c_loaded, 32)
            A(csig[:, :], crow[:, :], ACT.Sigmoid).then_inc(csig_ready, 1)
            for t in range(NC + 1):
                m = P if t < NC else TS
                act.wait_ge(x_loaded[t % XBUF], 16 * (t // XBUF + 1))
                wait(act, x_squared, t)
                A(xsq[0:m, 0:D], xrow[t % XBUF][0:m, :], ACT.Square, accum_out=ms9[0:m, t:t + 1]).then_inc(x_squared, 1)
            act.wait_ge(lb_in, 1)
            A(lbs[:, 0, :], lbs[:, 0, :], ACT.Exp)
            A(lbs[:, 1, :], lbs[:, 1, :], ACT.Exp).then_inc(lb_exp, 1)
            act.wait_ge(ms_ready, 1)
            root(NINE, rms_root)
            hi(Idx(0))

            def shift_and_round(buf, n, m, hi_out, col, full, count, ready):
                act.wait_ge(full, count)
                bias = mod[:, col, 0:1]
                A(hi_out[:, 0:n], buf[:, 0:n], ACT.Identity, bias=bias)
                if m > n:
                    A(hi_out[:, n:m], buf[:, n:m], ACT.Copy)
                A(buf[:, 0:n], buf[:, 0:n], ACT.Identity, bias=bias).then_inc(ready, 1)

            for j in range(NJ):
                shift_and_round(hbuf[j % 3], TP, T, h_hi[:, j, :], SH1 * NJ + j, h_full, j + 1, h_hi_ready)

            def tile_read(kind, h, t, before):
                if not (t.i is None and t.n < 0):
                    act.wait_ge(block_done, t.v + 1)
                z, bias = z3(t.par), column(V_BIN + kind * NJ, h.v)
                if kind == SA:
                    wait(act, gate_ready, h.v)
                    A(g3(ta[:, :]), z, ACT.Identity, bias=bias).then_inc(zfree(t)[0], 1)
                elif kind == SB:
                    A(g3(tb[:, :]), z, ACT.Sigmoid, bias=bias).then_inc(zfree(t)[0], 1)
                elif kind == SV:
                    if before is not None:
                        act.wait_ge(fill_done, (before + N_MISC).v + 1)
                    A(g3(v[:, :]), z, ACT.Identity, bias=bias).then_inc(zfree(t)[0], 1)
                elif kind == SQ:
                    act.wait_ge(u_ready, h.v + 1)
                    A(g3(tb[:, :]), z, ACT.Sigmoid, bias=bias).then_inc(sig_ready, 1)
                elif kind == SF:
                    A(g3(ta[:, :]), z, ACT.Sigmoid, bias=bias).then_inc(zfree(t)[0], 1)
                elif kind == SOG:
                    act.wait_ge(*zfree(t + (-2)))
                    A(g3(tb[:, :]), z, ACT.Sigmoid, bias=bias).then_inc(sig_ready, 1)
                elif kind == SGA:
                    act.wait_ge(fk_ready, h.v + 1)
                    A(g3(ta[:, :]), z, ACT.Sigmoid, bias=bias).then_inc(zfree(t)[0], 1)

            def squares(fill):
                act.wait_ge(fill_evac, fill.v + 1)
                A(sqp[:, :], O[:, 0:TP], ACT.Square)
                A(sqs[:, :], O[:, TP:T], ACT.Square).then_inc(square_ready, 1)

            def rec_root(fill):
                act.wait_ge(fill_evac, fill.v + 1)
                root(NINE, root_ready)

            def body(h, t0, f, rec):
                for j in range(NT):
                    hi(t0 + (j + 1))
                    if j:
                        tile_read(ORDER[j - 1], h, t0 + (j - 1), f if rec else None)
                    elif rec:
                        tile_read(SGA, h + (-1), t0 + (-1), None)
                    if j == 5 and rec:
                        squares(f + N_OS)
                        rec_root(f + N_SS)

            heads(act, body, lambda: None)

            vq = (v, q)

            def gate_b(n):
                t = Idx(ZT + n)
                act.wait_ge(block_done, t.n + 1)
                if n == 0:
                    act.wait_ge(gate_ready, NJ)
                wait(act, gb_stored[n % 2], 16 * (n // 2))
                A(g3(tab[n % 2][:, :]), z3(t.par), ACT.Sigmoid, bias=column(V_BIN + SGB * NJ, n)) \
                    .then_inc(zfree(t)[0], 1)

            def ln_square(j):
                act.wait_ge(centred, j + 1)
                wait(act, ln_added, j - 2)
                if j in (1, 2):
                    act.wait_ge(fill_done, rec7(N_SATT).n + 1)
                A(vq[j % 2][:, :] if j else ysum[:, :], yb[:, j, :], ACT.Square).then_inc(ln_squared, 1)

            for j in range(NJ):
                hi(Idx(ZT + j + 1))
                if j == 0:
                    tile_read(SGA, Idx(NJ - 1), Idx(ZT - 1), None)
                else:
                    gate_b(j - 1)
                if j == 4:
                    for n in range(4):
                        ln_square(n)
                if j == 5:
                    squares(rec7(N_OS))
                    for n in range(4, NJ):
                        ln_square(n)
                    rec_root(rec7(N_SS))
                if j == 6:
                    act.wait_ge(fill_evac, REC7 + LAST_AT[("lnss", 0)] + 1)
                    root(NINE, ln_root)
            gate_b(NJ - 1)

            def ln_apply(j):
                w, b = vec[:, V_LNW + j:V_LNW + j + 1], vec[:, V_LNB + j:V_LNB + j + 1]
                act.wait_ge(ln_scaled, j + 1)
                wait(act, ln_done, j - 1)
                A(vq[j % 2][:, :], yb[:, j, :], ACT.Sigmoid, bias=b, scale=w)
                A(yb[:, j, :], yb[:, j, :], ACT.Identity, bias=b, scale=w).then_inc(ln_affine, 1)

            hi(Idx(Z_OUT + 1))
            for m in range(NJ):
                ln_apply(m)
                act.wait_ge(m_loaded[m % 2], 16 * (m // 2 + 1))
                if m == 0:
                    act.wait_ge(block_done, Z_OUT)
                A(m_hi[0][:, m, :], mraw[m % 2][:, :], ACT.Copy).then_inc(m_hi_ready, 1)
            for m in range(NJ):
                act.wait_ge(m_prod, m + 1)
                A(m_hi[1][:, m, :], mraw[m % 2][:, :], ACT.Copy).then_inc(m_hi_ready, 1)

            with act.Fori(0, NJ // 2) as i:
                for n in range(2):
                    ft = Idx(n, i, 2)
                    for kk in range(2):
                        hi(Idx(Z_OUT + 2 + 2 * n + kk, i, 4))
                    act.wait_ge(*zfree(Idx(Z_OUT + n, i, 2)))
                    A(tab[n][:, :], at_head(x2, ft.v), ACT.Square).then_inc(x2_squared, 1)
            act.wait_ge(fill_evac, R_X2 + 1)
            root(NINE, x2_root)
            for j in range(NJ):
                shift_and_round(tab[j % 2], GW, GW, h2_hi[:, j, 0:GW], SH2 * NJ + j, h2_full, j + 1, h2_hi_ready)
            act.wait_ge(h2_ready, NJ)

            for g in range(G):
                if g:
                    act.wait_ge(y_stored[0], 32 * g)
                    act.wait_ge(y_stored[1], 16 * g)
                with act.Fori(0, NF // 2) as i:
                    for n in range(2):
                        t = Idx(T_FFN + T_GRP * g + n, i, 2)
                        b = Idx(B_FFN + B_GRP * g + 2 * n, i, 4)
                        fi = Idx(n, i, 2)
                        sg, a = ta[:, n * GW:(n + 1) * GW], tb[:, n * GW:(n + 1) * GW]
                        hi(b + 2)
                        A(sg, Z[t.par][:, 0, 0:GW], ACT.Sigmoid).then_inc(g_sig, 1)
                        hi(b + 3)
                        act.wait_ge(*zfree(t))
                        A(act_hi[:, ds(fi.v, 1), :].rearrange("p o t -> p (o t)"), a, ACT.Copy).then_inc(a_hi_ready, 1)

                def ffn_out(n, i, last_pass):
                    per = 0 if i is None else 2
                    j = Idx(n, i, per)
                    b = Idx(B_FFN + B_GRP * g + 2 * NF + 3 * n, i, 3 * per)
                    t = Idx(T_FFN + T_GRP * g + NF + n, i, per)
                    for kk in range(3):
                        if not (last_pass and 3 * n + kk + 2 >= 3 * NJ):
                            hi(b + (kk + 2), OUT_K[(kk + 2) % 3])
                    act.wait_ge(*zfree(t))
                    x = x2[:, ds(j.v, 1), g * GW:(g + 1) * GW].rearrange("p o t -> p (o t)")
                    A(tb[:, n % 2 * GW:(n % 2 + 1) * GW], x, ACT.Square).then_inc(x3_squared, 1)

                with act.Fori(0, NJ // 2 - (g == G - 1)) as i:
                    for n in range(2):
                        ffn_out(n, i, False)
                if g == G - 1:
                    for n in range(NJ - 2, NJ):
                        ffn_out(n, None, True)
                act.wait_ge(fill_evac, R_Y + R_Y_GRP * g + 1)
                root(((P, slice(0, 2)), (GW - 2 * P, slice(2, 3))), y_root)

        @block.gpsimd
        def _(pool):
            Q = nc.gpsimd
            st = Steps(pool, gchain, met)

            def low(b):
                pool.wait_ge(w_hi_ready, b.v + 1)
                st.tell(Q.tensor_tensor(w_lo[b.par][:, :, :], w_raw[b.par][:, :, :], w_hi[b.par][:, :, :].bitcast(F32),
                                        ALU.subtract), w_split, b.v + 1)

            st.tell(Q.memset(ones[:, :], 1.0), const_ready, 1)
            st.do(Q.memset(ident[:, :], 0.0))
            st.settle()
            st.tell(Q.affine_select(out=ident[:, :], in_=ident[:, :], compare_op=ALU.not_equal, fill=1.0, base=0,
                                    pattern=[[-1, P]], channel_multiplier=1), const_ready, 2)
            low(Idx(0))
            for j in range(NJ):
                pool.wait_ge(h_hi_ready, j + 1)
                st.tell(Q.tensor_tensor(h_lo[:, j, :], hbuf[j % 3][:, 0:T], h_hi[:, j, :].bitcast(F32), ALU.subtract),
                        h_ready, j + 1)

            pool.wait_ge(h_ready, NJ)
            pool.wait_ge(adaw_used, 8)
            pool.wait_ge(x_squared, NC + 1)
            pool.wait_ge(ht_stored, 16)
            pool.wait_ge(xt_stored, 16)
            for buf in (up[:, 0:HIST], att[:, :, :], att_s[:, :], smask[:, :, :].bitcast(F32)):
                st.do(Q.memset(buf, 0.0))
            for buf in (masks[:, :, :].bitcast(F32), bmask[:, :]):
                st.do(Q.memset(buf, 1.0))

            def select(ap, op, fill, base, pattern, channel):
                st.settle()
                st.do(Q.affine_select(out=ap, in_=ap, compare_op=op, fill=fill, base=base, pattern=pattern,
                                      channel_multiplier=channel))

            for lv in range(LV):
                b = 1 << lv
                ap = masks[:, lv, :].bitcast(F32)
                select(ap, ALU.is_ge, 0.0, 0, [[-2 * b, HB // b], [0, b]], 1)
                select(ap, ALU.is_ge, 0.0, b - 1, [[2 * b, HB // b], [0, b]], -1)
            one = smask[:, 0, :].bitcast(F32)
            select(one, ALU.not_equal, 1.0, 0, [[-1, TS]], 1)
            one = smask[:, 1, :].bitcast(F32).rearrange("p (n two) -> p n two", two=2)[:, :, 1]
            select(one, ALU.not_equal, 1.0, 0, [[-2, TS // 2]], 1)
            one = smask[:, 2, :].bitcast(F32).rearrange("p (n four) -> p n four", four=4)[:, :, 2:4]
            st.do(Q.memset(one, 1.0))
            select(one, ALU.is_ge, 0.0, 0, [[-4, NS], [0, 2]], 1)
            select(one, ALU.is_ge, 0.0, 1, [[4, NS], [0, 2]], -1)
            select(bmask[:, :], ALU.is_ge, 0.0, 0, [[-LS, NS]], 1)
            st.settle()
            st.tell(Q.affine_select(out=bmask[:, :], in_=bmask[:, :], compare_op=ALU.is_ge, fill=0.0, base=LS - 1,
                                    pattern=[[LS, NS]], channel_multiplier=-1), masks_ready, 1)
            st.restart()

            def gates(h, t0):
                pool.wait_ge(*zfree(t0 + (-2)))
                pool.wait_ge(*zfree(t0 + (-1)))
                wait(pool, operands_ready, NREADY * (h.v - 1))
                st.tell(Q.tensor_tensor(gate[:, :], ta[:, :], tb[:, :], ALU.mult), gate_ready, h.v)

            def channel_sum(h):
                pool.wait_ge(conv_done, h.v)
                y = at_head(yb, h.v - 1)
                if h.i is None and h.n == 1:
                    st.tell(Q.tensor_copy(ysum[:, :], y), ysum_ready, 1)
                else:
                    pool.wait_ge(ysum_ready, h.v - 1)
                    st.tell(Q.tensor_tensor(ysum[:, :], ysum[:, :], y, ALU.add), ysum_ready, h.v)

            def glu(h, t0, f, rec):
                pool.wait_ge(*zfree(t0 + 1))
                wait(pool, conv_done, h.v)
                if rec:
                    pool.wait_ge(fill_done, (f + N_MISC).v + 1)
                st.do(Q.tensor_tensor(up[:, HIST:UT], ta[:, 0:TP], tb[:, 0:TP], ALU.mult))
                st.do(Q.tensor_tensor(us[:, :, HIST:US], seqs(ta[:, TP:T]), seqs(tb[:, TP:T]), ALU.mult))
                st.do(Q.tensor_tensor(tail[:, 0:HIST], ta[:, TP - HIST:TP], tb[:, TP - HIST:TP], ALU.mult))
                st.tell(Q.tensor_tensor(tail[:, HIST:HIST + TS], ta[:, TP:T], tb[:, TP:T], ALU.mult), u_ready, h.v + 1)

            def body(h, t0, f, rec):
                for j in range(NT):
                    low(t0 + (j + 1))
                    if j == 0 and rec:
                        gates(h, t0)
                    if j == 1 and rec:
                        channel_sum(h)
                    if j == 2:
                        glu(h, t0, f, rec)

            heads(pool, body, st.restart)

            vq = (v, q)
            for j in range(NJ):
                low(Idx(ZT + j + 1))
                if j == 0:
                    gates(Idx(NJ), Idx(ZT))
                    channel_sum(Idx(NJ))
                if j in (2, 3):
                    if j == 2:
                        pool.wait_ge(fill_evac, REC7 + LAST_AT[("mu", 2)] + 1)
                    for n in range(4 * (j - 2), 4 * (j - 1)):
                        st.tell(Q.tensor_tensor(yb[:, n, :], yb[:, n, :], murow[:, :], ALU.subtract), centred, n + 1)
                if j in (4, 5):
                    for n in range(1, 4) if j == 4 else range(4, NJ):
                        pool.wait_ge(ln_squared, n + 1)
                        if n > 1:
                            pool.wait_ge(ln_added, n - 1)
                        st.tell(Q.tensor_tensor(ysum[:, :], ysum[:, :], vq[n % 2][:, :], ALU.add), ln_added, n)
            low(Idx(Z_OUT + 1))
            for n in range(NJ):
                pool.wait_ge(ln_affine, n + 1)
                st.tell(Q.tensor_tensor(yb[:, n, :], yb[:, n, :], vq[n % 2][:, :], ALU.mult), ln_done, n + 1)
            st.settle()

            for m in range(NJ, 2 * NJ):
                pool.wait_ge(m_loaded[m % 2], 16 * (m // 2 + 1))
                st.tell(Q.tensor_tensor(mraw[m % 2][:, :], mraw[m % 2][:, :], yb[:, m - NJ, :], ALU.mult),
                        m_prod, m - NJ + 1)
            for b in range(Z_OUT + 2, B_FFN):
                low(Idx(b))

            for j in range(NJ):
                pool.wait_ge(h2_hi_ready, j + 1)
                st.tell(Q.tensor_tensor(h2_lo[:, j, 0:GW], tab[j % 2][:, 0:GW], h2_hi[:, j, 0:GW].bitcast(F32),
                                        ALU.subtract), h2_ready, j + 1)
            pool.wait_ge(fill_evac, R_X2 + 1 + len(ROW_PARTS))
            for g in range(1, G):
                for j in range(NJ):
                    a, b = g * GW, (g + 1) * GW
                    n = min(b, TP) - a
                    sec = SH2 * NJ + j
                    st.settle()
                    st.do(Q.tensor_tensor(h2buf[:, :], x2[:, j, a:b], ysum[:, a:b], ALU.mult))
                    st.settle()
                    st.do(Q.tensor_scalar(h2buf[:, 0:n], h2buf[:, 0:n], am[:, j, 0:1], mod[:, sec, 0:1],
                                          ALU.mult, ALU.add))
                    if n < GW:
                        s = seqs(h2buf[:, n:GW])
                        st.do(Q.tensor_tensor(s, s, per_seq(am[:, j, 1:NSEQ]), ALU.mult))
                        st.settle()
                        st.do(Q.tensor_tensor(s, s, per_seq(mod[:, sec, 1:NSEQ]), ALU.add))
                    st.settle()
                    st.do(Q.tensor_copy(h2_hi[:, j, a:b], h2buf[:, :]))
                    st.settle()
                    st.tell(Q.tensor_tensor(h2_lo[:, j, a:b], h2buf[:, :], h2_hi[:, j, a:b].bitcast(F32),
                                            ALU.subtract), h2_ready, NJ * g + j + 1)


_INS = ("x_prompt", "x_sample", "state_hgrn", "state_conv", "c_prompt", "c_sample", "w_ada", "b_ada", "norm_mix_w",
        "w_in", "b_in", "lb_logits", "hgrn_norm_w", "conv_dw_w", "conv_dw_b", "conv_ln_w", "conv_ln_b", "w_out",
        "norm_ffn_w", "w_ffn_in", "w_ffn_out", "norm_final_w")
_OUTS = ((1, TP, D), (NS, LS, D), (1, 1, NJ, P, P), (1, 1, HIST, D), (1, NS, NJ, P, P), (1, NS, HIST, D))


def kernel(**inputs):
    import numpy as _np
    import concourse.bacc as _bacc
    from concourse.bass_utils import run_bass_kernel_spmd as _run

    nc = _bacc.Bacc("TRN2", target_bir_lowering=False, num_devices=1)
    arrays, args = {}, []
    for name in _INS:
        a = _np.ascontiguousarray(inputs[name])
        arrays[f"in_{name}_dram"] = a
        args.append(nc.dram_tensor(f"in_{name}_dram", a.shape, F32, kind="ExternalInput").ap())
    for n, shape in enumerate(_OUTS):
        args.append(nc.dram_tensor(f"out_{n}_dram", shape, F32, kind="ExternalOutput").ap())
    program(nc, *args)
    r = _run(nc, [arrays], core_ids=[0])
    return tuple(r.results[0][f"out_{n}_dram"] for n in range(len(_OUTS)))
```

```python
from contextlib import ExitStack

import concourse.bass as bass
from concourse import mybir

F32, F32R, I32 = mybir.dt.float32, mybir.dt.float32r, mybir.dt.int32
ACT = mybir.ActivationFunctionType
ALU = mybir.AluOpType
ds = bass.ds

P = 128
D = 1024
NJ = D // P
TP = 1024
NS, LS = 8, 4
TS = NS * LS
T = TP + TS
G, GW = 3, T // 3
NC = TP // P
LV = 7
HB = P // 2
TAPS = 31
HIST = TAPS - 1
UT = HIST + TP
US = HIST + LS
FF = 2816
NF = FF // P
NSEQ = 1 + NS
EPS = 1e-6

SQ, SF, SV, SOG, SA, SB, SGA, SGB = range(8)
ORDER = (SA, SB, SV, SQ, SF, SOG, SGA)
NT = len(ORDER)
SH1, SC1, G1, SH2, SC2, G2 = range(6)
NADA = 4

V_BIN, V_MIX, V_HN, V_DWB, V_LNW, V_LNB, V_FFN, V_FIN = 0, 64, 72, 80, 88, 96, 104, 112
NVA = 120
V_ADA, V_LB0, V_LB1 = NVA, NVA + 48, NVA + 56
NVB = 64
V_DW = NVA + NVB
NDW = TAPS * NJ
NVEC = V_DW + NDW

N_VT0, N_VT1, N_MISC, N_DG0, N_DG1, N_LV = range(6)
(N_SATT, N_KT0, N_KT1, N_KTS, N_KV0, N_KV1, N_O0, N_O1, N_OS, N_KVS0, N_SS, N_KVS1, N_R0, N_R1, N_R2) = range(12, 27)
NFILL = 27
SLOTS = 4
ADA_AT = {N_MISC: 0, N_SATT: 1, N_KTS: 2, N_OS: 3}
ADA_BACK = {N_SATT: 0, N_KTS: 1, N_OS: 2, N_SS: 3}
ADA_COL, BACK_COL = 384, 368
NREADY = LV + 3
R_START, R_LEVEL, R_VBLK, R_RMS = 1, 2, LV + 2, LV + 3
CONV_SLOT = 10

REC7 = NFILL * (NJ - 1)
LAST = ([("rec", n) for n in range(5)] + [("mu", n) for n in range(3)] + [("rec", n) for n in range(5, 20)]
        + [("lnss", 0)] + [("rec", 20)] + [("lnr", n) for n in range(3)]
        + [("rec", n) for n in range(21, NFILL)])
LAST_AT = {step: n for n, step in enumerate(LAST)}
LAST_AFTER = (1, 3, 5, 7, 7)
R_X2 = REC7 + len(LAST)
R_Y = R_X2 + 4
R_Y_GRP = 1 + 1 + 2 * 3

ZT = NT * NJ
Z_OUT = ZT + NJ
B_FFN = Z_OUT + 2 * NJ
T_FFN = Z_OUT + NJ
B_GRP = 2 * NF + 3 * NJ
T_GRP = NF + NJ
OUT_K = (8, 8, NF - 16)
TAIL_AT = {f: n for n, f in enumerate((0, 2, 4, 5, 7, 8, 10, 11))}
STORE_AT = (7, 10, 13)
PEELED = 14
CHUNKS = tuple((c * P, min(P, GW - c * P)) for c in range((GW + P - 1) // P))

P0_C, P0_VEC, P0_X = 0, 1, 2
P0_HIST = P0_X + 2 * (NC + 1)
P0_ADA = P0_HIST + 4
P0_ROWS = P0_ADA + 1
N0 = P0_ROWS + 3
XBUF = 4
MBUF = 4
ROW_PARTS = ((0, 512), (512, 512), (1024, TS))


class Idx:

    def __init__(self, n, i=None, per=0):
        assert per % 2 == 0
        self.n, self.i, self.per = n, i, per

    def __add__(self, m):
        return Idx(self.n + m, self.i, self.per)

    @property
    def v(self):
        return self.n if self.i is None else self.i * self.per + self.n

    @property
    def half(self):
        return self.n // 2 if self.i is None else self.i * (self.per // 2) + self.n // 2

    @property
    def par(self):
        return self.n % 2


def wait(eng, sem, value):
    if isinstance(value, int) and value <= 0:
        return
    eng.wait_ge(sem, value)


def fill_in_slot(s):
    if s == N_R0:
        return None
    n = s - (s > N_R0)
    return n if n < NFILL else None


def heads(eng, body, end):
    for h in range(2):
        body(Idx(h), Idx(NT * h), Idx(NFILL * (h - 1)), h >= 1)
        end()
    with eng.Fori(1, NJ // 2) as i:
        for h in range(2):
            body(Idx(h, i, 2), Idx(NT * h, i, 2 * NT), Idx(NFILL * (h - 1), i, 2 * NFILL), True)
            end()


def wait_apart(eng, met, sem, value):
    if isinstance(value, int):
        wait(eng, sem, value)
        return
    value = eng.to_reg(value)
    eng.wait_ge(*met)
    eng.wait_ge(sem, value)


class Steps:

    def __init__(self, eng, chain, met):
        self.eng, self.chain, self.n, self.last, self.met = eng, chain, 0, None, met

    def do(self, ins):
        ins.then_inc(self.chain, 1)
        self.n += 1
        self.last = (self.chain, self.n)

    def tell(self, ins, sem, value):
        ins.then_inc(sem, 1)
        self.last = (sem, value)

    def settle(self):
        if self.last:
            self.eng.wait_ge(*self.last)

    def settle_apart(self):
        if self.last:
            wait_apart(self.eng, self.met, *self.last)

    def restart(self):
        self.settle_apart()
        if self.n:
            self.eng.sem_clear(self.chain)
        self.n, self.last = 0, None


def program(nc, x_prompt, x_sample, state_hgrn, state_conv, c_prompt, c_sample, w_ada, b_ada, norm_mix_w, w_in, b_in,
            lb_logits, hgrn_norm_w, conv_dw_w, conv_dw_b, conv_ln_w, conv_ln_b, w_out, norm_ffn_w, w_ffn_in,
            w_ffn_out, norm_final_w, y_prompt, y_sample, st_prompt, cv_prompt, st_sample, cv_sample):
    ctx = ExitStack()

    win_v, wada_v, wout_v, wfi_v, wfo_v = (
        w[0].rearrange("(k p) n -> p k n", p=P) for w in (w_in, w_ada, w_out, w_ffn_in, w_ffn_out))
    merged = nc.dram_tensor("merged_scratch", (2 * NJ, P, T), F32, kind="Internal").ap()
    xt_dram = nc.dram_tensor("xt_scratch", (NJ, P, T), F32, kind="Internal").ap()
    hist_dram = nc.dram_tensor("hist_scratch", (NJ, P, NS * HIST), F32, kind="Internal").ap()

    def at(name, shape, dt, offset):
        return nc.alloc_sbuf_tensor_at(name, shape, dt, offset=offset)

    class Place:
        def __init__(self, start, end):
            self.p, self.end, self.where = start, end, {}

        def __call__(self, name, shape, dt=F32):
            n = 4
            for s in shape[1:]:
                n *= s
            self.where[name] = self.p
            t = at(name, shape, dt, self.p)
            self.p += (n + 31) // 32 * 32
            assert self.p <= self.end, (name, self.p, self.end)
            return t

    EIGHT = NJ * T * 4
    A1 = 16512
    A2, B1, C1, C2, WR = (A1 + n * EIGHT for n in range(1, 6))
    DD, END = WR + 6 * 4096, nc.sbuf_usable_end

    h_hi, h_lo = at("h_hi", [P, NJ, T], F32R, A1), at("h_lo", [P, NJ, T], F32R, A2)
    xt = at("xt", [P, NJ, T], F32, B1)
    yb = at("yb", [P, NJ, T], F32, B1)
    m_lo = [at("m_lo_a", [P, NJ, T], F32R, A1), at("m_lo_b", [P, NJ, T], F32R, A2)]
    m_hi = [at("m_hi_a", [P, NJ, T], F32R, C1), at("m_hi_b", [P, NJ, T], F32R, B1)]
    x2 = at("x2", [P, NJ, T], F32, C2)
    h2_hi, h2_lo = at("h2_hi", [P, NJ, T], F32R, A1), at("h2_lo", [P, NJ, T], F32R, A2)
    act_hi, act_lo = at("act_hi", [P, NF, GW], F32R, B1), at("act_lo", [P, NF, GW], F32R, B1 + NF * GW * 4)
    h2buf = at("h2buf", [P, GW], F32, B1 + 2 * NF * GW * 4)
    ystage = at("ystage", [P, D], F32, B1 + (2 * NF + 1) * GW * 4)
    w_raw = [at(f"w_raw{i}", [P, 8, P], F32, WR + i * 4096) for i in range(2)]
    w_hi = [at(f"w_hi{i}", [P, 8, P], F32R, WR + (2 + i) * 4096) for i in range(2)]
    w_lo = [at(f"w_lo{i}", [P, 8, P], F32R, WR + (4 + i) * 4096) for i in range(2)]

    d = Place(DD, END)
    ta, tb = d("ta", [P, T]), d("tb", [P, T])
    tab = (ta, tb)
    ysum = d("ysum", [P, T])
    vec = d("vec", [P, NVEC])
    mod = d("mod", [P, 6 * NJ, NSEQ])
    ct = d("ct", [P, NJ, NSEQ])
    ident, ones = d("ident", [P, P]), d("ones", [P, 1])
    am = d("am", [P, NJ, NSEQ])
    lbs = d("lbs", [P, 4, NJ])
    ms9, rs9 = d("ms9", [P, NC + 1]), d("rs9", [P, NC + 1])

    r = Place(C1, WR)
    att = r("att", [P, NC, P])
    vtok, ktok = r("vtok", [P, NC, P]), r("ktok", [P, NC, P])
    S, S0 = r("S", [P, NC, P]), r("S0", [P, NS, P])
    k, qd, f = (r(n, [P, T]) for n in ("k", "qd", "f"))
    sqs, k0s, k1s, q0s, q1s = (r(n, [P, TS]) for n in ("sqs", "k0s", "k1s", "q0s", "q1s"))
    assert r.p <= C2
    r.p = C2
    q, v = r("q", [P, T]), r("v", [P, T])
    tot = r("tot", [P, T])
    up, us = r("up", [P, UT]), r("us", [P, NS, US])
    O, gate, aw = r("O", [P, T]), r("gate", [P, T]), r("aw", [P, 8, P])
    tail = r("tail", [P, HIST + TS])
    att_s = r("att_s", [TS, TS])
    vtok_s, ktok_s = r("vtok_s", [TS, P]), r("ktok_s", [TS, P])
    urow = r("urow", [HIST + TS, P])
    smask, bmask = r("smask", [TS, 3, TS], I32), r("bmask", [TS, NS])
    masks = d("masks", [P, LV, HB], I32)
    arow = r("arow", [NSEQ, P])
    sqp = at("sqp", [P, TP], F32, r.where["vtok"])
    vblk = at("vblk", [TS, NS, P], F32, r.where["ktok"])
    mraw = [at(f"mraw{i}", [P, T], F32, r.where[n]) for i, n in enumerate(("up", "gate", "tot", "O"))]
    murow = at("murow", [P, T], F32, r.where["up"])

    e = Place(C1, WR)
    ada_w = [e(f"ada_w{i}", [P, 8, 2 * P]) for i in range(2)]
    xrow = [e(f"xrow{i}", [P, D]) for i in range(XBUF)]
    hrow = e("hrow", [NS // 2 * HIST, 2, D])
    ht = e("ht", [P, NJ, NS * HIST])
    crow, csig = e("crow", [NSEQ, D]), e("csig", [NSEQ, D])
    vrow = e("vrow", [P, 4, P])
    xsq = e("xsq", [P, T])
    hbuf = (ta, tb, xsq)

    Z = [ctx.enter_context(nc.psum_tensor(f"Z{i}", [P, G, 512], F32)) for i in range(2)]
    R = [ctx.enter_context(nc.psum_tensor(f"R{i}", [P, 512], F32)) for i in range(2)]

    def sem(name):
        return ctx.enter_context(nc.semaphore(name))

    def two(name):
        return [sem(f"{name}{i}") for i in range(2)]

    w_loaded = two("w_loaded")
    w_hi_ready, w_split = sem("w_hi_ready"), sem("w_split")
    block_done = sem("block_done")
    z_free = two("z_free")
    fill_done, fill_evac = sem("fill_done"), sem("fill_evac")
    operands_ready, sig_ready, fk_ready = sem("operands_ready"), sem("sig_ready"), sem("fk_ready")
    gate_ready, u_ready, conv_done, ysum_ready = sem("gate_ready"), sem("u_ready"), sem("conv_done"), sem("ysum_ready")
    hist_loaded, square_ready, root_ready = sem("hist_loaded"), sem("square_ready"), sem("root_ready")
    s0_loaded, s0_stored, state_stored = sem("s0_loaded"), sem("s0_stored"), sem("state_stored")
    m_stored, u_stored, ada_loaded = sem("m_stored"), sem("u_stored"), sem("ada_loaded")
    masks_ready = sem("masks_ready")
    const_ready = sem("const_ready")
    met = (const_ready, 2)
    vchain, gchain = sem("vchain"), sem("gchain")
    rows_loaded, c_loaded, hrow_loaded, hist_copied = (
        sem("rows_loaded"), sem("c_loaded"), sem("hrow_loaded"), sem("hist_copied"))
    x_loaded = [sem(f"x_loaded{i}") for i in range(XBUF)]
    adaw_loaded, adaw_used, adaw_read = two("adaw_loaded"), sem("adaw_used"), sem("adaw_read")
    csig_ready, c_ready, x_squared = (
        sem("csig_ready"), sem("c_ready"), sem("x_squared"))
    p0_done, p0_evac = sem("p0_done"), sem("p0_evac")
    ms_ready, rms_root, rms_ready = sem("ms_ready"), sem("rms_root"), sem("rms_ready")
    lb_in, lb_exp = sem("lb_in"), sem("lb_exp")
    h_full, h_hi_ready, h_ready = sem("h_full"), sem("h_hi_ready"), sem("h_ready")
    xt_stored, ht_stored = sem("xt_stored"), sem("ht_stored")
    centred, ln_squared, ln_added, ln_root, ln_recip = (
        sem("centred"), sem("ln_squared"), sem("ln_added"), sem("ln_root"), sem("ln_recip"))
    ln_scaled, ln_affine, ln_done = sem("ln_scaled"), sem("ln_affine"), sem("ln_done")
    gb_stored = two("gb_stored")
    m_loaded = [sem(f"m_loaded{i}") for i in range(MBUF)]
    m_prod, m_hi_ready, m_split = sem("m_prod"), sem("m_hi_ready"), sem("m_split")
    xr_loaded, x2_squared, x2_summed = two("xr_loaded"), sem("x2_squared"), sem("x2_summed")
    x2_root, x2_recip = sem("x2_root"), sem("x2_recip")
    h2_full, h2_hi_ready, h2_ready = sem("h2_full"), sem("h2_hi_ready"), sem("h2_ready")
    g_sig, a_hi_ready, a_ready = sem("g_sig"), sem("a_hi_ready"), sem("a_ready")
    x3_squared, x3_summed, y_root, y_recip = sem("x3_squared"), sem("x3_summed"), sem("y_root"), sem("y_recip")
    y_staged = sem("y_staged")
    y_stored = two("y_stored")

    def zfree(tile):
        return z_free[tile.par], tile.half + 1

    def loaded(b):
        return w_loaded[b.par], (b.half + 1) * 16

    def z3(par):
        return Z[par][:, :, 0:GW]

    def g3(ap):
        return ap.rearrange("p (g n) -> p g n", g=G)

    def at_head(tensor, h):
        return tensor[:, ds(h, 1), :].rearrange("p o t -> p (o t)")

    def at_hidden(tensor, f):
        return tensor[:, ds(f.v, 1), :].rearrange("p o t -> p (o t)")

    def column(base, h):
        return vec[:, ds(base + h, 1)]

    def seqs(ap):
        return ap.rearrange("p (s t) -> p s t", t=LS)

    def per_seq(ap):
        return ap.unsqueeze(2).to_broadcast([P, NS, LS])

    def lbcol(row, h):
        return lbs[:, row, ds(h, 1)]

    def halves(ap, b, which):
        return ap.rearrange("p (n two b) -> p n two b", two=2, b=b)[:, :, which, :]

    T_AT = (None, 0, T // 2, T // 2 + T // 4, T // 2 + T // 4 + 128, T // 2 + T // 4 + 192,
            T // 2 + T // 4 + 224, T // 2 + T // 4 + 240)

    def totals(l):
        n = (T, T // 2, T // 4, 128, 64, 32, 16, 8)[l]
        return f[:, 0:T] if l == 0 else tot[:, T_AT[l]:T_AT[l] + n]

    def p0_bank(n):
        return Z[n // 3 % 2][:, n % 3, :]

    def rec7(n):
        return Idx(REC7 + LAST_AT[("rec", n)])

    with ctx:
        block = ctx.enter_context(nc.Block())

        @block.sync
        def _(sp):
            def load_block(b, src, n=8):
                wait_apart(sp, met, w_split, b.v if b.i is None and b.n < 2 else (b + (-1)).v)
                sp.dma_start(w_raw[b.par][:, 0:n, :], src).then_inc(w_loaded[b.par], 16)

            sp.dma_start(crow[0:1, :], c_prompt).then_inc(c_loaded, 16)
            sp.dma_start(crow[1:NSEQ, :], c_sample).then_inc(c_loaded, 16)

            def load_x(t):
                if t >= XBUF:
                    sp.wait_ge(x_squared, t - XBUF + 1)
                    sp.wait_ge(p0_done, P0_X + 2 * (t - XBUF + 1))
                n = P if t < NC else TS
                src = x_prompt[0, t * P:(t + 1) * P, :] if t < NC else x_sample.rearrange("s t d -> (s t) d")
                sp.dma_start(xrow[t % XBUF][0:n, :], src).then_inc(x_loaded[t % XBUF], 16)

            def load_ada_cols(n):
                if n >= 2:
                    sp.wait_ge(adaw_used, n - 1)
                sp.dma_start(ada_w[n % 2][:, :, :], wada_v[:, :, n * 2 * P:(n + 1) * 2 * P]) \
                    .then_inc(adaw_loaded[n % 2], 16)

            load_x(0)
            load_x(1)

            def rows(row, tile, src):
                sp.dma_start(vrow[row:row + src.shape[0], tile, :], src).then_inc(rows_loaded, 16)

            for row, w in ((V_BIN, b_in), (V_MIX, norm_mix_w), (V_HN, hgrn_norm_w), (V_DWB, conv_dw_b),
                           (V_LNW, conv_ln_w), (V_LNB, conv_ln_b), (V_FFN, norm_ffn_w)):
                rows(row, 0, w[0].rearrange("(r c) -> r c", c=P))
            rows(V_FIN, 0, norm_final_w.rearrange("(r c) -> r c", c=P))
            rows(0, 1, b_ada[0].rearrange("(r c) -> r c", c=P))
            rows(V_LB0 - NVA, 1, lb_logits.rearrange("l (r c) -> (l r) c", c=P))
            taps = conv_dw_w[0].rearrange("t (r c) -> (t r) c", c=P)
            for n in range(2):
                rows(0, 2 + n, taps[n * NDW // 2:(n + 1) * NDW // 2, :])
            load_ada_cols(0)
            load_x(2)
            load_ada_cols(1)
            load_x(3)
            old = state_conv[0].rearrange("(two s) w d -> two (s w) d", two=2)
            for m in range(2):
                sp.dma_start(hrow[:, m, :], old[m]).then_inc(hrow_loaded, 16)
            for n in range(2, 8):
                load_ada_cols(n)
                if n + 2 <= NC:
                    load_x(n + 2)
            for b in range(2):
                load_block(Idx(b), win_v[:, :, ORDER[b] * D:ORDER[b] * D + P])
            sp.dma_start(cv_sample[0, :, 0:HIST - LS, :], state_conv[0, :, LS:HIST, :]).then_inc(hist_copied, 16)
            sp.wait_ge(p0_evac, P0_ROWS)
            sp.dma_start(hist_dram.rearrange("j p w -> p j w"), ht[:, :, :]).then_inc(ht_stored, 16)
            sp.dma_start(xt_dram.rearrange("j p t -> p j t"), xt[:, :, :]).then_inc(xt_stored, 16)
            sp.wait_ge(ht_stored, 16)
            sp.wait_ge(xt_stored, 16)
            sp.wait_ge(x_squared, NC + 1)
            sp.wait_ge(h_ready, NJ)
            sp.wait_ge(adaw_used, 8)

            def load_ada(hh, p):
                sp.dma_start(aw[:, :, :], wada_v[:, :, ds(hh.v * P + (G1 + p) * D, P)]).then_inc(ada_loaded, 16)

            def store_urow(hh, fill):
                wait_apart(sp, met, fill_evac, fill.v + 1)
                sp.dma_start(cv_prompt[0, 0, :, ds(hh.v * P, P)], urow[0:HIST, :]).then_inc(u_stored, 16)
                sp.dma_start(cv_sample[0, :, HIST - LS:HIST, ds(hh.v * P, P)], urow[HIST:HIST + TS, :]) \
                    .then_inc(u_stored, 16)

            def store_state(hh, fill):
                wait_apart(sp, met, fill_evac, fill.v + 1)
                sp.dma_start(st_prompt[0, 0, ds(hh.v, 1), :, :].rearrange("o k v -> (o k) v"), S[:, NC - 1, :]) \
                    .then_inc(state_stored, 16)

            def store_s0(hh, fill):
                sp.wait_ge(fill_evac, fill.v + 1)
                sp.dma_start(st_sample[0, :, ds(hh.v, 1), :, :].rearrange("s o k v -> k (s o) v"), S0[:, :, :]) \
                    .then_inc(s0_stored, 16)

            def load_s0(hh):
                wait(sp, s0_stored, hh.v * 16)
                sp.dma_start(S0[:, :, :], state_hgrn[0, :, ds(hh.v, 1), :, :].rearrange("s o k v -> k (s o) v")) \
                    .then_inc(s0_loaded, 16)

            def store_o(hh, fill):
                sp.wait_ge(fill_evac, fill.v + 1)
                sp.dma_start(merged[ds(hh.v, 1), :, :].rearrange("o p t -> (o p) t"), O[:, :]).then_inc(m_stored, 16)

            def ada_after(n, hh, fill):
                sp.wait_ge(fill_done, fill.v + 1)
                p = ADA_AT[n] + 1
                if p < NADA:
                    load_ada(hh, p)
                else:
                    load_ada(hh + 1, 0)

            def recurrence_io(j, hh, f, before, f_before):
                if before is not None:
                    if j == 0:
                        ada_after(N_OS, before, f_before + N_OS)
                    if j == 1:
                        store_s0(before, f_before + N_KVS1)
                        store_o(before, f_before + N_R2)
                if hh is not None:
                    if j == 2:
                        load_s0(hh)
                        store_urow(hh, f + N_MISC)
                        ada_after(N_MISC, hh, f + N_MISC)
                    if j == 5:
                        ada_after(N_SATT, hh, f + N_SATT)
                    if j == 6:
                        ada_after(N_KTS, hh, f + N_KTS)
                        store_state(hh, f + N_KV1)

            def body(h, t0, f, rec):
                for j in range(NT):
                    load_block(t0 + j, win_v[:, :, ds(h.v * P + ORDER[j] * D, P)]) if not (
                        h.i is None and h.n == 0 and j < 2) else None
                    if j == 1:
                        wait(sp, conv_done, h.v)
                        sp.dma_start(us[:, :, 0:HIST], hist_dram[ds(h.v, 1), :, :].rearrange(
                            "o p (s w) -> (o p) s w", w=HIST)).then_inc(hist_loaded, 16)
                        if not rec:
                            load_ada(h, 0)
                    early = h.i is None and h.n < 2
                    recurrence_io(j, h + (-1) if rec else None, f,
                                  None if early else h + (-2), None if early else f + (-NFILL))

            heads(sp, body, lambda: None)

            h7 = Idx(NJ - 1)
            for j in range(NJ):
                load_block(Idx(ZT + j), win_v[:, :, SGB * D + j * P:SGB * D + (j + 1) * P])
                recurrence_io(j, None, None, Idx(NJ - 2), Idx(REC7 - NFILL))
                if j == 2:
                    load_s0(h7)
                    store_urow(h7, rec7(N_MISC))
                    ada_after(N_MISC, h7, rec7(N_MISC))
                if j == 6:
                    ada_after(N_KTS, h7, rec7(N_KTS))
                if j >= 3:
                    sp.wait_ge(*zfree(Idx(ZT + j - 3)))
                    sp.dma_start(merged[NJ + j - 3], tab[(j - 3) % 2][:, :]).then_inc(gb_stored[(j - 3) % 2], 16)
                if j == 5:
                    ada_after(N_SATT, h7, rec7(N_SATT))
                if j == 7:
                    store_state(h7, rec7(N_KV1))

            def load_m(m):
                wait(sp, m_split, m - MBUF + 1)
                sp.dma_start(mraw[m % MBUF][:, :], merged[m]).then_inc(m_loaded[m % MBUF], 16)

            sp.wait_ge(m_stored, 16 * (NJ - 1))
            sp.wait_ge(centred, NJ)
            load_m(0)
            for b in range(2):
                load_block(Idx(Z_OUT + b), wout_v[:, b * 8:b * 8 + 8, 0:P])
                j = NJ - 3 + b
                sp.wait_ge(*zfree(Idx(ZT + j)))
                sp.dma_start(merged[NJ + j], tab[j % 2][:, :]).then_inc(gb_stored[j % 2], 16)
            store_s0(h7, rec7(N_KVS1))
            sp.wait_ge(operands_ready, NREADY * NJ)
            load_m(1)
            load_m(2)
            store_o(h7, rec7(N_R2))
            sp.wait_ge(m_stored, 16 * NJ)
            load_m(3)
            load_m(4)
            load_m(5)
            j = NJ - 1
            sp.wait_ge(*zfree(Idx(ZT + j)))
            sp.dma_start(merged[NJ + j], tab[j % 2][:, :]).then_inc(gb_stored[j % 2], 16)
            for m in range(6, NJ):
                load_m(m)
            for i in range(2):
                sp.wait_ge(gb_stored[i], 16 * NJ // 2)
            sp.wait_ge(u_stored, 32 * NJ)

            def load_residual(j):
                wait(sp, x2_summed, (j + (-1)).v)
                sp.dma_start(tab[j.par][:, :], xt_dram[ds(j.v, 1), :, :].rearrange("o p t -> (o p) t")) \
                    .then_inc(xr_loaded[j.par], 16)

            def load_out_tile(ft):
                for kk in range(2):
                    load_block(Idx(Z_OUT + 2 * ft.n + kk, ft.i, 2 * ft.per),
                               wout_v[:, kk * 8:kk * 8 + 8, ds(ft.v * P, P)])

            for m in range(NJ, NJ + MBUF):
                load_m(m)
            load_out_tile(Idx(1))
            for m in range(NJ + MBUF, 2 * NJ):
                load_m(m)
            for n in range(2):
                load_residual(Idx(n))
            load_out_tile(Idx(2))
            load_out_tile(Idx(3))
            with sp.Fori(1, NJ // 2 - 1) as i:
                for n in range(2):
                    load_residual(Idx(n, i, 2))
                for n in range(2):
                    load_out_tile(Idx(2 + n, i, 2))
            for n in range(2):
                load_residual(Idx(NJ - 2 + n))

            def ffn_in_block(g, f, kk):
                load_block(Idx(B_FFN + B_GRP * g + 2 * f.n + kk, f.i, 2 * f.per),
                           wfi_v[:, :, ds(f.v * P + kk * FF, P)])

            def store_y(g, c):
                c0, m = CHUNKS[c]
                sp.wait_ge(fill_evac, R_Y + R_Y_GRP * g + 2 * c + 4)
                t0 = g * GW + c0
                src, left = (ystage, y_staged) if g < G - 1 else (tab[c % 2], y_stored[c % 2])
                n = min(m, TP - t0)
                sp.dma_start(y_prompt[0, t0:t0 + n, :], src[0:n, 0:D]).then_inc(left, 16)
                if n < m:
                    sp.dma_start(y_sample.rearrange("s t d -> (s t) d"), src[n:m, 0:D]).then_inc(left, 16)

            for g in range(G):
                peeled = PEELED if g else 2
                for f in range(peeled):
                    for kk in range(2):
                        ffn_in_block(g, Idx(f), kk)
                    if g and f in STORE_AT:
                        store_y(g - 1, STORE_AT.index(f))
                with sp.Fori(peeled // 2, NF // 2) as i:
                    for n in range(2):
                        for kk in range(2):
                            ffn_in_block(g, Idx(n, i, 2), kk)
                with sp.Fori(0, NJ // 2) as i:
                    for n in range(2):
                        for kk in range(3):
                            load_block(Idx(B_FFN + B_GRP * g + 2 * NF + 3 * n + kk, i, 6),
                                       wfo_v[:, 8 * kk:8 * kk + OUT_K[kk], ds((i * 2 + n) * P, P)], OUT_K[kk])
            for c in range(len(CHUNKS)):
                store_y(G - 1, c)
            sp.wait_ge(y_staged, 16 * (G - 1) * len(CHUNKS))
            sp.wait_ge(y_stored[0], 16 * 3)
            sp.wait_ge(y_stored[1], 16)
            sp.wait_ge(hist_copied, 16)
            sp.wait_ge(s0_stored, 16 * NJ)
            sp.wait_ge(state_stored, 16 * NJ)
            sp.wait_ge(u_stored, 32 * NJ)

        @block.tensor
        def _(pe):
            mm, transpose = nc.tensor.matmul, nc.tensor.transpose

            pe.wait_ge(const_ready, 2)

            def fill0(n):
                if n >= 6:
                    pe.wait_ge(p0_evac, n - 5)
                return p0_bank(n)

            pe.wait_ge(c_ready, 1)
            bank = fill0(P0_C)
            for j in range(NJ):
                last = transpose(bank[:, j * NSEQ:(j + 1) * NSEQ], crow[:, j * P:(j + 1) * P], ident[0:NSEQ, 0:NSEQ])
            last.then_inc(p0_done, 1)
            pe.wait_ge(rows_loaded, 16 * 12)
            bank, col = fill0(P0_VEC), 0
            for tile, n in enumerate((NVA, NVB, NDW // 2, NDW // 2)):
                last = transpose(bank[:, col:col + n], vrow[0:n, tile, :], ident[0:n, 0:n])
                col += n
            last.then_inc(p0_done, 1)

            def ada_cols(n):
                pe.wait_ge(adaw_loaded[n % 2], 16 * (n // 2 + 1))
                if n >= 2:
                    pe.wait_ge(adaw_read, n - 1)
                for kt in range(NJ):
                    last = mm(R[n % 2][0:NSEQ, 0:2 * P], ct[:, kt, :], ada_w[n % 2][:, kt, :],
                              start=kt == 0, stop=kt == NJ - 1)
                last.then_inc(adaw_used, 1)

            pe.wait_ge(p0_evac, P0_C + 1)
            for t in range(NC + 1):
                pe.wait_ge(x_loaded[t % XBUF], 16 * (t // XBUF + 1))
                m = P if t < NC else TS
                for hf in range(2):
                    bank = fill0(P0_X + 2 * t + hf)
                    for j in range(4):
                        last = transpose(bank[:, j * m:(j + 1) * m],
                                         xrow[t % XBUF][0:m, (4 * hf + j) * P:(4 * hf + j + 1) * P], ident[0:m, 0:m])
                    last.then_inc(p0_done, 1)
                if t < 8:
                    ada_cols(t)
            pe.wait_ge(hrow_loaded, 32)
            m = NS // 2 * HIST
            for n in range(4):
                bank = fill0(P0_HIST + n)
                for j in range(2):
                    for row_tile in range(2):
                        c = (2 * j + row_tile) * m
                        last = transpose(bank[:, c:c + m], hrow[:, row_tile, (2 * n + j) * P:(2 * n + j + 1) * P],
                                         ident[0:m, 0:m])
                last.then_inc(p0_done, 1)
            bank = fill0(P0_ADA)
            pe.wait_ge(adaw_read, 8)
            for j in range(2 * NJ):
                last = transpose(bank[:, j * NSEQ:(j + 1) * NSEQ],
                                 tab[j // NJ][0:NSEQ, j % NJ * P:(j % NJ + 1) * P], ident[0:NSEQ, 0:NSEQ])
            last.then_inc(p0_done, 1)
            pe.wait_ge(rms_ready, 1)
            for n, (t0, w) in enumerate(ROW_PARTS):
                bank = fill0(P0_ROWS + n)
                for c in range(0, w, P):
                    m = min(P, w - c)
                    last = mm(bank[:, c:c + m], rs9[0:m, (t0 + c) // P:(t0 + c) // P + 1].to_broadcast([m, P]),
                              ident[0:m, 0:m], start=True, stop=True)
                last.then_inc(p0_done, 1)

            def products(b, outs, n, hi, lo, first, last_block, at_slot=None, slots=(), before_row=None):
                whi, wlo = w_hi[b.par], w_lo[b.par]
                pe.wait_ge(w_split, b.v + 1)
                for kt in range(n):
                    if before_row is not None:
                        before_row(kt)
                    for m, (w, x) in enumerate(((whi, hi), (whi, lo), (wlo, hi))):
                        for g, out in enumerate(outs):
                            last = mm(out, w[:, kt, :], x(kt, g), start=first and kt == 0 and m == 0,
                                      stop=last_block and kt == n - 1 and m == 2)
                    if kt == n - 1:
                        last.then_inc(block_done, 1)
                    for s in range(slots.count(kt)):
                        at_slot()

            def z_tile(b, at_slot=None, slots=(), before_row=None):
                t = b
                if t.i is None and t.n < 2:
                    pe.wait_ge(p0_evac, N0)
                else:
                    pe.wait_ge(*zfree(t + (-2)))
                products(b, [Z[t.par][:, g, 0:GW] for g in range(G)], NJ,
                         lambda kt, g: h_hi[:, kt, g * GW:(g + 1) * GW], lambda kt, g: h_lo[:, kt, g * GW:(g + 1) * GW],
                         True, True, at_slot, slots, before_row)

            def small(fill):
                if not (fill.i is None and fill.n < 2):
                    pe.wait_ge(fill_evac, (fill + (-1)).v)
                return R[fill.par]

            def tr(out, in_, m):
                return transpose(out, in_, ident[0:m, 0:m])

            def ada(bank, hh, p):
                pe.wait_ge(ada_loaded, (hh.v * NADA + (p + 1)) * 16)
                for kt in range(NJ):
                    last = mm(bank[0:NSEQ, ADA_COL:ADA_COL + P], ct[:, kt, :], aw[:, kt, :], start=kt == 0,
                              stop=kt == NJ - 1)
                return last

            def rows_of(bank, t0, w, recips):
                for c in range(0, w, P):
                    m = min(P, w - c)
                    i = (t0 + c) // P
                    last = mm(bank[:, c:c + m], recips[0:m, i:i + 1].to_broadcast([m, P]), ident[0:m, 0:m],
                              start=True, stop=True)
                return last

            def rec_fill(n, hh, fill, of):
                def ready(m):
                    pe.wait_ge(operands_ready, hh.v * NREADY + m)

                def read(m):
                    pe.wait_ge(fill_evac, of(m).v + 1)

                bank = small(fill)
                if n in (N_VT0, N_VT1):
                    if n == N_VT0:
                        pe.wait_ge(*zfree(Idx(NT * hh.n + ORDER.index(SV), hh.i, NT * hh.per)))
                    for c in range(4):
                        cc = c + 4 * (n - N_VT0)
                        last = tr(bank[:, c * P:(c + 1) * P], v[:, cc * P:(cc + 1) * P], P)
                elif n == N_MISC:
                    pe.wait_ge(u_ready, hh.v + 1)
                    tr(bank[0:TS, 0:P], v[:, TP:T], P)
                    last = tr(bank[0:HIST + TS, P:2 * P], tail[:, :], P)
                elif n in (N_DG0, N_DG1):
                    ready(R_START)
                    for c in range(4):
                        cc = (c + 4 * (n - N_DG0)) * P
                        last = mm(bank[:, c * P:(c + 1) * P], k[:, cc:cc + P], q[:, cc:cc + P], start=True, stop=True)
                elif N_LV <= n < N_LV + LV:
                    lv = n - N_LV
                    ready(R_START if lv == 0 else R_LEVEL + lv - 1)
                    for c in range(NC):
                        last = mm(bank[:, c * HB:(c + 1) * HB], k[:, c * P:(c + 1) * P],
                                  halves(qd[:, c * P:(c + 1) * P], 1 << lv, 1), start=True, stop=True)
                elif n == N_SATT:
                    ready(R_LEVEL + 1)
                    mm(bank[0:TS, 0:TS], k0s[:, :], q[:, TP:T], start=True, stop=True)
                    mm(bank[0:TS, TS:2 * TS], k0s[:, :], q0s[:, :], start=True, stop=True)
                    last = mm(bank[0:TS, 2 * TS:3 * TS], k1s[:, :], q1s[:, :], start=True, stop=True)
                elif n in (N_KT0, N_KT1):
                    ready(R_LEVEL + LV - 1)
                    for c in range(4):
                        cc = c + 4 * (n - N_KT0)
                        last = tr(bank[:, c * P:(c + 1) * P], k[:, cc * P:(cc + 1) * P], P)
                elif n == N_KTS:
                    last = tr(bank[0:TS, 0:P], k[:, TP:T], P)
                elif n in (N_KV0, N_KV1):
                    read(N_KT0 + n - N_KV0)
                    for c in range(4):
                        cc = c + 4 * (n - N_KV0)
                        last = mm(bank[:, c * P:(c + 1) * P], ktok[:, cc, :], vtok[:, cc, :], start=True, stop=True)
                elif n in (N_O0, N_O1):
                    read(N_KV0 + n - N_O0)
                    for c in range(4):
                        cc = c + 4 * (n - N_O0)
                        out = bank[:, c * P:(c + 1) * P]
                        last = mm(out, vtok[:, cc, :], att[:, cc, :], start=True, stop=cc == 0)
                        if cc:
                            last = mm(out, S[:, cc - 1, :], qd[:, cc * P:(cc + 1) * P], start=False, stop=True)
                elif n == N_OS:
                    pe.wait_ge(s0_loaded, (hh.v + 1) * 16)
                    mm(bank[:, 0:TS], vtok_s[:, :], att_s[:, :], start=True, stop=False)
                    for s in range(NS):
                        last = mm(bank[:, s * LS:(s + 1) * LS], S0[:, s, :], qd[:, TP + s * LS:TP + (s + 1) * LS],
                                  start=False, stop=s == NS - 1)
                elif n in (N_KVS0, N_KVS1):
                    hf = 0 if n == N_KVS0 else 1
                    ready(R_VBLK)
                    last = mm(bank[:, :], ktok_s[:, :], vblk[:, 4 * hf:4 * hf + 4, :], start=True, stop=True)
                elif n == N_SS:
                    pe.wait_ge(square_ready, hh.v + 1)
                    for c in range(NC):
                        mm(bank[:, c:c + 1], sqp[:, c * P:(c + 1) * P], ones[:, :], start=True, stop=True)
                    last = mm(bank[0:TS, NC:NC + 1], sqs[:, :], ones[:, :], start=True, stop=True)
                else:
                    if n == N_R0:
                        ready(R_RMS)
                    last = rows_of(bank, *ROW_PARTS[n - N_R0], rs9)
                if n in ADA_BACK:
                    last = tr(bank[:, BACK_COL:BACK_COL + NSEQ], arow[:, :], NSEQ)
                if n in ADA_AT:
                    last = ada(bank, hh, ADA_AT[n])
                last.then_inc(fill_done, 1)

            def token_sums(bank, row, n):
                for c in range(0, n, P):
                    m = min(P, n - c)
                    last = mm(bank[0:m, c // P:c // P + 1], row[:, c:c + m], ones[:, :], start=True, stop=True)
                return last

            def body(h, t0, f, rec):
                at = [0]

                def slot():
                    n = fill_in_slot(at[0])
                    if rec and n is not None:
                        rec_fill(n, h + (-1), f + n, lambda m: f + m)
                    at[0] += 1

                for j in range(NT):
                    first = h.i is None and h.n == 0 and j == 0
                    z_tile(t0 + j, slot, (1, 3, 5, 7), (lambda kt: pe.wait_ge(h_ready, kt + 1)) if first else None)

            heads(pe, body, lambda: None)

            at = [0]

            def last_slot():
                n = at[0]
                at[0] += 1
                if n >= len(LAST):
                    return
                kind, m = LAST[n]
                fill = Idx(REC7 + n)
                if kind == "rec":
                    rec_fill(m, Idx(NJ - 1), fill, rec7)
                    return
                bank = small(fill)
                if kind == "mu":
                    if m == 0:
                        pe.wait_ge(ysum_ready, NJ)
                    t0, w = ROW_PARTS[m]
                    last = mm(bank[:, 0:w], ones[:, :].to_broadcast([P, P]), ysum[:, t0:t0 + w], start=True, stop=True)
                elif kind == "lnss":
                    pe.wait_ge(ln_added, NJ - 1)
                    last = token_sums(bank, ysum, T)
                else:
                    if m == 0:
                        pe.wait_ge(ln_recip, 1)
                    last = rows_of(bank, *ROW_PARTS[m], rs9)
                last.then_inc(fill_done, 1)

            for j in range(NJ):
                z_tile(Idx(ZT + j), last_slot, LAST_AFTER)

            def out_tile(ft):
                t = Idx(Z_OUT + ft.n, ft.i, ft.per)
                pe.wait_ge(*zfree(t + (-2)))
                for kk in range(2):
                    b = Idx(Z_OUT + 2 * ft.n + kk, ft.i, 2 * ft.per)
                    products(b, [Z[t.par][:, g, 0:GW] for g in range(G)], NJ,
                             lambda kt, g: m_hi[kk][:, kt, g * GW:(g + 1) * GW],
                             lambda kt, g: m_lo[kk][:, kt, g * GW:(g + 1) * GW], kk == 0, kk == 1,
                             before_row=lambda kt: pe.wait_ge(m_split, kk * NJ + kt + 1))

            with pe.Fori(0, NJ // 2) as i:
                for n in range(2):
                    out_tile(Idx(n, i, 2))

            fill = Idx(R_X2)
            bank = small(fill)
            pe.wait_ge(x2_summed, NJ)
            token_sums(bank, ysum, T).then_inc(fill_done, 1)
            for n, (t0, w) in enumerate(ROW_PARTS):
                bank = small(fill + (1 + n))
                if n == 0:
                    pe.wait_ge(x2_recip, 1)
                rows_of(bank, t0, w, rs9).then_inc(fill_done, 1)

            def tail_fill(g, n):
                fill = R_Y + R_Y_GRP * g
                bank = small(Idx(fill + n))
                if n == 0:
                    pe.wait_ge(x3_summed, NJ * (g + 1))
                    last = token_sums(bank, ysum, GW)
                elif n == 1:
                    pe.wait_ge(y_recip, g + 1)
                    last = rows_of(bank, 0, GW, rs9)
                else:
                    if n == 2:
                        pe.wait_ge(fill_evac, fill + 2)
                    (c0, m), hf = CHUNKS[(n - 2) // 2], n % 2
                    for j in range(4):
                        last = tr(bank[0:m, j * P:(j + 1) * P], x2[:, 4 * hf + j, g * GW + c0:g * GW + c0 + m], P)
                last.then_inc(fill_done, 1)

            for g in range(G):
                cols = slice(g * GW, (g + 1) * GW)

                def in_tile(f, beside=None):
                    t = Idx(T_FFN + T_GRP * g + f.n, f.i, f.per)
                    pe.wait_ge(*zfree(t + (-2)))
                    for kk in range(2):
                        products(Idx(B_FFN + B_GRP * g + 2 * f.n + kk, f.i, 2 * f.per), [Z[t.par][:, kk, 0:GW]], NJ,
                                 lambda kt, _: h2_hi[:, kt, cols], lambda kt, _: h2_lo[:, kt, cols], True, True,
                                 before_row=(lambda kt: pe.wait_ge(h2_ready, kt + 1)) if g == 0 else None)
                        if kk == 0 and beside is not None:
                            tail_fill(g - 1, beside)

                if g:
                    pe.wait_ge(h2_ready, NJ * (g + 1))
                peeled = PEELED if g else 0
                for f in range(peeled):
                    in_tile(Idx(f), TAIL_AT.get(f))
                with pe.Fori(peeled // 2, NF // 2) as i:
                    for n in range(2):
                        in_tile(Idx(n, i, 2))

                def hidden(kk):
                    return lambda kt: pe.wait_ge(a_ready, NF * g + 8 * kk + kt + 1)

                with pe.Fori(0, NJ // 2) as i:
                    for n in range(2):
                        t = Idx(T_FFN + T_GRP * g + NF + n, i, 2)
                        pe.wait_ge(*zfree(t + (-2)))
                        for kk in range(3):
                            products(Idx(B_FFN + B_GRP * g + 2 * NF + 3 * n + kk, i, 6), [Z[t.par][:, 0, 0:GW]],
                                     OUT_K[kk], lambda kt, _: act_hi[:, 8 * kk + kt, :],
                                     lambda kt, _: act_lo[:, 8 * kk + kt, :], kk == 0, kk == 2,
                                     before_row=hidden(kk) if n == 0 else None)
            for n in range(R_Y_GRP):
                tail_fill(G - 1, n)

        @block.vector
        def _(dve):
            V = nc.vector
            st = Steps(dve, vchain, met)

            dve.wait_ge(c_loaded, 32)
            dve.wait_ge(csig_ready, 1)
            st.tell(V.tensor_tensor(crow[:, :], crow[:, :], csig[:, :], ALU.mult), c_ready, 1)

            def evac0(n, out, in_):
                dve.wait_ge(p0_done, n + 1)
                st.tell(V.tensor_copy(out, in_), p0_evac, n + 1)

            evac0(P0_C, ct[:, :, :], p0_bank(P0_C)[:, 0:NJ * NSEQ].rearrange("p (j s) -> p j s", s=NSEQ))
            evac0(P0_VEC, vec[:, :], p0_bank(P0_VEC)[:, 0:NVEC])
            def scales(sec, w):
                st.settle()
                st.do(V.tensor_scalar(am[:, :, :], mod[:, sec * NJ:(sec + 1) * NJ, :], 1.0, None, ALU.add))
                st.settle()
                st.do(V.tensor_tensor(am[:, :, :], am[:, :, :], vec[:, w:w + NJ].unsqueeze(2).to_broadcast(
                    [P, NJ, NSEQ]), ALU.mult))

            l0, l1 = vec[:, V_LB0:V_LB0 + NJ], vec[:, V_LB1:V_LB1 + NJ]
            st.settle()
            st.do(V.tensor_tensor(lbs[:, 3, :], l0, l1, ALU.max))
            st.settle()
            st.do(V.tensor_tensor(lbs[:, 0, :], l0, lbs[:, 3, :], ALU.subtract))
            st.tell(V.tensor_tensor(lbs[:, 1, :], l1, lbs[:, 3, :], ALU.subtract), lb_in, 1)
            for t in range(NC + 1):
                m = P if t < NC else TS
                for hf in range(2):
                    n = P0_X + 2 * t + hf
                    evac0(n, xt[:, 4 * hf:4 * hf + 4, t * P:t * P + m],
                          p0_bank(n)[:, 0:4 * m].rearrange("p (j t) -> p j t", j=4))
                if t < 8:
                    dve.wait_ge(adaw_used, t + 1)
                    st.tell(V.tensor_copy(tab[t // 4][0:NSEQ, t % 4 * 2 * P:(t % 4 + 1) * 2 * P],
                                          R[t % 2][0:NSEQ, 0:2 * P]),
                            adaw_read, t + 1)
            dve.wait_ge(x_squared, NC + 1)
            st.do(V.tensor_scalar(ms9[:, 0:NC], ms9[:, 0:NC], 1.0 / D, EPS, ALU.mult, ALU.add))
            st.tell(V.tensor_scalar(ms9[0:TS, NC:NC + 1], ms9[0:TS, NC:NC + 1], 1.0 / D, EPS, ALU.mult, ALU.add),
                    ms_ready, 1)
            for n in range(4):
                evac0(P0_HIST + n, ht[:, 2 * n:2 * n + 2, :].rearrange("p j w -> p (j w)"),
                      p0_bank(P0_HIST + n)[:, 0:2 * NS * HIST])
            dve.wait_ge(p0_done, P0_ADA + 1)
            st.tell(V.tensor_tensor(mod[:, 0:2 * NJ, :],
                                    p0_bank(P0_ADA)[:, 0:2 * NJ * NSEQ].rearrange("p (j s) -> p j s", s=NSEQ),
                                    vec[:, V_ADA:V_ADA + 2 * NJ].unsqueeze(2).to_broadcast([P, 2 * NJ, NSEQ]),
                                    ALU.add), p0_evac, P0_ADA + 1)
            scales(SC1, V_MIX)
            dve.wait_ge(lb_exp, 1)
            st.do(V.tensor_tensor(lbs[:, 3, :], lbs[:, 0, :], lbs[:, 1, :], ALU.add))
            st.settle()
            st.do(V.reciprocal(lbs[:, 3, :], lbs[:, 3, :]))
            st.settle()
            st.do(V.tensor_tensor(lbs[:, 0, :], lbs[:, 0, :], lbs[:, 3, :], ALU.mult))
            st.settle()
            st.do(V.tensor_scalar(lbs[:, 1, :], lbs[:, 0, :], -1.0, 1.0, ALU.mult, ALU.add))
            st.do(V.tensor_scalar(lbs[:, 2, :], lbs[:, 0, :], 1.0, None, ALU.subtract))
            dve.wait_ge(rms_root, 1)
            st.do(V.reciprocal(rs9[:, 0:NC], rs9[:, 0:NC]))
            st.tell(V.reciprocal(rs9[0:TS, NC:NC + 1], rs9[0:TS, NC:NC + 1]), rms_ready, 1)
            for n, (t0, w) in enumerate(ROW_PARTS):
                evac0(P0_ROWS + n, ysum[:, t0:t0 + w], p0_bank(P0_ROWS + n)[:, 0:w])
            def modulate(out, x, row, j, shift, t0, t1, full, count):
                n = min(t1, TP) - t0
                ins = V.scalar_tensor_tensor(out[:, 0:n], x[:, 0:n], am[:, j, 0:1], row[:, 0:n], ALU.mult, ALU.mult)
                if t1 <= TP:
                    st.tell(ins, full, count)
                    return
                st.do(ins)
                s = seqs(out[:, n:n + TS])
                st.do(V.tensor_tensor(s, seqs(x[:, n:n + TS]), seqs(row[:, n:n + TS]), ALU.mult))
                st.settle()
                st.do(V.tensor_tensor(s, s, per_seq(am[:, j, 1:NSEQ]), ALU.mult))
                st.settle()
                st.tell(V.tensor_tensor(s, s, per_seq(mod[:, shift * NJ + j, 1:NSEQ]), ALU.add), full, count)

            st.settle()
            for j in range(NJ):
                wait(dve, h_ready, j - 2)
                modulate(hbuf[j % 3][:, 0:T], xt[:, j, :], ysum[:, :], j, SH1, 0, T, h_full, j + 1)
            dve.wait_ge(h_ready, NJ)
            dve.wait_ge(xt_stored, 16)
            dve.wait_ge(ht_stored, 16)
            st.restart()

            def rec_start(hh):
                st.settle()
                st.do(V.tensor_tensor(qd[:, :], q[:, :], f[:, :], ALU.mult))
                st.do(V.tensor_copy(k0s[:, :], k[:, TP:T]))
                st.settle()
                st.tell(V.tensor_copy(q0s[:, :], qd[:, TP:T]), operands_ready, hh.v * NREADY + R_START)

            def rec_totals():
                for lv in range(1, LV + 1):
                    if lv > 1:
                        st.settle()
                    below = totals(lv - 1)[:, 0:2 * (TP >> lv) if lv > 2 else None]
                    n = (TP >> lv) + ((TS >> lv) if lv <= 2 else 0)
                    pairs = below[:, 0:2 * n].rearrange("p (n two) -> p n two", two=2)
                    st.do(V.tensor_tensor(totals(lv)[:, 0:n], pairs[:, :, 0], pairs[:, :, 1], ALU.mult))

            def level_up(lv, hh):
                b = 1 << lv
                n = T if lv <= 1 else TP
                pairs = totals(lv)[:, 0:n >> lv].rearrange("p (n two) -> p n two", two=2)
                shape = [P, n // (2 * b), b]
                late, early = halves(qd[:, 0:n], b, 1), halves(k[:, 0:n], b, 0)
                st.do(V.tensor_tensor(late, late, pairs[:, :, 0:1].to_broadcast(shape), ALU.mult))
                st.tell(V.tensor_tensor(early, early, pairs[:, :, 1:2].to_broadcast(shape), ALU.mult),
                        operands_ready, hh.v * NREADY + R_LEVEL + lv)
                if lv == 0:
                    st.settle()
                    st.do(V.tensor_copy(q1s[:, :], qd[:, TP:T]))
                    st.do(V.tensor_copy(k1s[:, :], k[:, TP:T]))
                    st.settle()

            def rec_evac(n, hh, fill):
                bank = R[fill.par]
                done = (fill_evac, fill.v + 1)

                def four(ap):
                    return ap.rearrange("p (c n) -> p c n", c=4)

                if n in (N_DG0, N_DG1):
                    wait_apart(dve, met, fill_done, fill.v + 1)
                else:
                    dve.wait_ge(fill_done, fill.v + 1)
                if n in ADA_BACK:
                    sec = (G1 + ADA_BACK[n]) * NJ
                    st.do(V.tensor_scalar(mod[:, ds(sec + hh.v, 1), :].rearrange("p o s -> p (o s)"),
                                          bank[:, BACK_COL:BACK_COL + NSEQ], column(V_ADA + sec, hh.v), None, ALU.add))
                if n in ADA_AT:
                    st.do(V.tensor_copy(arow[:, :], bank[0:NSEQ, ADA_COL:ADA_COL + P]))
                if n in (N_VT0, N_VT1):
                    st.tell(V.tensor_copy(vtok[:, 4 * n:4 * n + 4, :], four(bank[:, :])), *done)
                    if n == N_VT0:
                        rec_start(hh)
                elif n == N_MISC:
                    if not (hh.i is None and hh.n == 0):
                        wait(dve, u_stored, hh.v * 32)
                    st.do(V.tensor_copy(vtok_s[:, :], bank[0:TS, 0:P]))
                    st.tell(V.tensor_copy(urow[:, :], bank[0:HIST + TS, P:2 * P]), *done)
                    rec_totals()
                elif n in (N_DG0, N_DG1):
                    c = 4 * (n - N_DG0)
                    st.settle_apart()
                    st.tell(V.copy_predicated(att[:, c:c + 4, :],
                                              ident[:, :].bitcast(I32).unsqueeze(1).to_broadcast([P, 4, P]),
                                              four(bank[:, :])), *done)
                elif N_LV <= n < N_LV + LV:
                    lv = n - N_LV
                    b = 1 << lv
                    level_up(lv, hh)
                    out = att[:, :, :].rearrange("p c (n two b) -> p c n two b", two=2, b=b)[:, :, :, 1, :]
                    data = bank[:, :].rearrange("p (c n b) -> p c n b", c=NC, b=b)
                    mask = masks[:, lv, :].rearrange("p (n b) -> p n b", b=b).unsqueeze(1).to_broadcast(
                        [P, NC, HB // b, b])
                    st.settle_apart()
                    st.tell(V.copy_predicated(out, mask, data), *done)
                elif n == N_SATT:
                    for m in range(3):
                        st.settle_apart()
                        ins = V.copy_predicated(att_s[:, :], smask[:, m, :], bank[0:TS, m * TS:(m + 1) * TS])
                        st.do(ins) if m < 2 else st.tell(ins, *done)
                elif n in (N_KT0, N_KT1):
                    c = 4 * (n - N_KT0)
                    st.tell(V.tensor_copy(ktok[:, c:c + 4, :], four(bank[:, :])), *done)
                elif n == N_KTS:
                    st.tell(V.tensor_copy(ktok_s[:, :], bank[0:TS, 0:P]), *done)
                elif n in (N_KV0, N_KV1):
                    if n == N_KV1:
                        wait(dve, state_stored, hh.v * 16)
                    for c in range(4):
                        cc = c + 4 * (n - N_KV0)
                        add = bank[:, c * P:(c + 1) * P]
                        if cc == 0:
                            st.do(V.tensor_copy(S[:, 0, :], add))
                            continue
                        st.settle()
                        ins = V.scalar_tensor_tensor(S[:, cc, :], S[:, cc - 1, :], totals(LV)[:, cc:cc + 1], add,
                                                     ALU.mult, ALU.add)
                        st.do(ins) if c < 3 else st.tell(ins, *done)
                    if n == N_KV1:
                        st.tell(V.tensor_tensor(vblk[:, :, :], vtok_s[:, :].unsqueeze(1).to_broadcast([TS, NS, P]),
                                                bmask[:, :].unsqueeze(2).to_broadcast([TS, NS, P]), ALU.mult),
                                operands_ready, hh.v * NREADY + R_VBLK)
                elif n in (N_O0, N_O1):
                    if n == N_O0:
                        wait(dve, m_stored, hh.v * 16)
                    c = 4 * P * (n - N_O0)
                    st.tell(V.tensor_copy(O[:, c:c + 4 * P], bank[:, :]), *done)
                elif n == N_OS:
                    st.tell(V.tensor_copy(O[:, TP:T], bank[:, 0:TS]), *done)
                elif n in (N_KVS0, N_KVS1):
                    for s in range(4):
                        seq = s + (0 if n == N_KVS0 else 4)
                        ins = V.scalar_tensor_tensor(S0[:, seq, :], S0[:, seq, :],
                                                     totals(2)[:, TP // 4 + seq:TP // 4 + seq + 1],
                                                     bank[:, s * P:(s + 1) * P], ALU.mult, ALU.add)
                        st.do(ins) if s < 3 else st.tell(ins, *done)
                    if n == N_KVS1:
                        dve.wait_ge(root_ready, hh.v + 1)
                        st.do(V.reciprocal(rs9[:, 0:NC], rs9[:, 0:NC]))
                        st.tell(V.reciprocal(rs9[0:TS, NC:NC + 1], rs9[0:TS, NC:NC + 1]), operands_ready,
                                hh.v * NREADY + R_RMS)
                elif n == N_SS:
                    st.do(V.tensor_scalar(ms9[:, 0:NC], bank[:, 0:NC], 1.0 / P, EPS, ALU.mult, ALU.add))
                    st.tell(V.tensor_scalar(ms9[0:TS, NC:NC + 1], bank[0:TS, NC:NC + 1], 1.0 / P, EPS, ALU.mult,
                                            ALU.add), *done)
                    dve.wait_ge(gate_ready, hh.v + 1)
                    st.do(V.scalar_tensor_tensor(O[:, :], O[:, :], column(V_HN, hh.v), gate[:, :], ALU.mult, ALU.mult))
                else:
                    t0, w = ROW_PARTS[n - N_R0]
                    st.settle()
                    st.tell(V.tensor_tensor(O[:, t0:t0 + w], O[:, t0:t0 + w], bank[:, 0:w], ALU.mult), *done)

            def conv_tap(n, h):
                y = yb[:, ds(h.v, 1), :].rearrange("p o t -> p (o t)")
                w = column(V_DW + n * NJ, h.v)
                yp, ys = y[:, 0:TP], seqs(y[:, TP:T])
                xp, xs = up[:, n:n + TP], us[:, :, n:n + LS]
                if n == 0:
                    dve.wait_ge(u_ready, h.v + 1)
                    dve.wait_ge(hist_loaded, (h.v + 1) * 16)
                    bias = column(V_DWB, h.v)
                    st.do(V.tensor_scalar(yp, xp, w, bias, ALU.mult, ALU.add))
                    st.do(V.tensor_scalar(ys, xs, w, bias, ALU.mult, ALU.add))
                    return
                st.settle()
                st.do(V.scalar_tensor_tensor(yp, xp, w, yp, ALU.mult, ALU.add))
                ins = V.scalar_tensor_tensor(ys, xs, w, ys, ALU.mult, ALU.add)
                if n < TAPS - 1:
                    st.do(ins)
                else:
                    st.tell(ins, conv_done, h.v + 1)

            def tile_read(j, h, t0):
                t = t0 + j
                kind = ORDER[j]
                if kind in (SQ, SOG):
                    dve.wait_ge(sig_ready, h.v * 2 + (1 if kind == SQ else 2))
                    out = q if kind == SQ else tb
                    st.tell(V.scalar_tensor_tensor(g3(out[:, :]), z3(t.par), column(V_BIN + kind * NJ, h.v),
                                                   g3(tb[:, :]), ALU.add, ALU.mult), *zfree(t))
                elif kind == SF:
                    dve.wait_ge(*zfree(t))
                    st.do(V.tensor_scalar(f[:, :], ta[:, :], lbcol(1, h.v), lbcol(0, h.v), ALU.mult, ALU.add))
                    st.tell(V.tensor_scalar(k[:, :], ta[:, :], lbcol(2, h.v), lbcol(1, h.v), ALU.mult, ALU.add),
                            fk_ready, h.v + 1)

            def body(h, t0, fl, rec):
                taps = iter(range(TAPS))
                hh = h + (-1)
                for j in range(NT):
                    if j:
                        tile_read(j - 1, h, t0)
                    for s in range(SLOTS):
                        slot = SLOTS * j + s
                        n = fill_in_slot(slot)
                        if n == 0 and rec and h.i is None:
                            dve.wait_ge(masks_ready, 1)
                        if rec and n is not None:
                            rec_evac(n, hh, fl + n)
                        if slot >= CONV_SLOT and n not in (N_OS, N_SS):
                            for tap in (next(taps, None), next(taps, None)):
                                if tap is not None:
                                    conv_tap(tap, h)

            heads(dve, body, st.restart)

            h7 = Idx(NJ - 1)

            def centre(j):
                st.settle()
                st.tell(V.tensor_tensor(yb[:, j, :], yb[:, j, :], murow[:, :], ALU.subtract), centred, j + 1)

            def scale(j):
                st.settle()
                st.tell(V.tensor_tensor(yb[:, j, :], yb[:, j, :], ysum[:, :], ALU.mult), ln_scaled, j + 1)

            to_centre, to_scale = iter(()), iter(())
            for n, (kind, m) in enumerate(LAST):
                fill = Idx(REC7 + n)
                bank = R[fill.par]
                if kind == "rec":
                    rec_evac(m, h7, fill)
                    for j in (next(to_centre, None),):
                        if j is not None:
                            centre(j)
                    for j in (next(to_scale, None), next(to_scale, None)):
                        if j is not None:
                            scale(j)
                    continue
                dve.wait_ge(fill_done, fill.n + 1)
                if kind == "mu":
                    t0, w = ROW_PARTS[m]
                    st.tell(V.tensor_scalar(murow[:, t0:t0 + w], bank[:, 0:w], 1.0 / D, None, ALU.mult),
                            fill_evac, fill.n + 1)
                    if m == 2:
                        dve.wait_ge(ysum_ready, NJ)
                        to_centre = iter(range(NJ))
                elif kind == "lnss":
                    st.do(V.tensor_scalar(ms9[:, 0:NC], bank[:, 0:NC], 1.0 / D, EPS, ALU.mult, ALU.add))
                    st.tell(V.tensor_scalar(ms9[0:TS, NC:NC + 1], bank[0:TS, NC:NC + 1], 1.0 / D, EPS, ALU.mult,
                                            ALU.add), fill_evac, fill.n + 1)
                    dve.wait_ge(ln_root, 1)
                    st.do(V.reciprocal(rs9[:, 0:NC], rs9[:, 0:NC]))
                    st.tell(V.reciprocal(rs9[0:TS, NC:NC + 1], rs9[0:TS, NC:NC + 1]), ln_recip, 1)
                else:
                    t0, w = ROW_PARTS[m]
                    st.tell(V.tensor_copy(ysum[:, t0:t0 + w], bank[:, 0:w]), fill_evac, fill.n + 1)
                    if m == 2:
                        to_scale = iter(range(NJ))
            def silu(j):
                dve.wait_ge(ln_affine, j + 1)
                st.tell(V.tensor_tensor(yb[:, j, :], yb[:, j, :], (v, q)[j % 2][:, :], ALU.mult), ln_done, j + 1)

            def merged_low(m):
                dve.wait_ge(m_hi_ready, m + 1)
                st.tell(V.tensor_tensor(m_lo[m // NJ][:, m % NJ, :], mraw[m % MBUF][:, :],
                                        m_hi[m // NJ][:, m % NJ, :].bitcast(F32), ALU.subtract), m_split, m + 1)

            for j in range(NJ // 2):
                silu(j)
            dve.wait_ge(block_done, Z_OUT)
            merged_low(0)
            silu(4)
            merged_low(1)
            for j in range(5, NJ):
                silu(j)
            for m in range(2, 2 * NJ):
                merged_low(m)
            st.settle()
            st.do(V.memset(ysum[:, :], 0.0))
            st.restart()

            def gated_add(out, base, psum, sec, j, t0, t1):
                n = min(t1, TP) - t0
                row = mod[:, ds(sec * NJ + j, 1), :].rearrange("p o s -> p (o s)")
                prompt = (out[:, 0:n], psum[:, 0:n], row[:, 0:1], base[:, 0:n], ALU.mult, ALU.add)
                if t1 <= TP:
                    return [lambda: V.scalar_tensor_tensor(*prompt)]
                so, sb, s = seqs(out[:, n:n + TS]), seqs(base[:, n:n + TS]), seqs(psum[:, n:n + TS])
                tmp = seqs(rowtmp[:, 0:TS])
                return [lambda: V.scalar_tensor_tensor(*prompt),
                        lambda: V.tensor_tensor(tmp, s, per_seq(row[:, 1:NSEQ]), ALU.mult),
                        lambda: V.tensor_tensor(so, sb, tmp, ALU.add)]

            rowtmp = masks[:, 0, :].bitcast(F32)

            def out_tile(ft):
                t = Idx(Z_OUT + ft.n, ft.i, ft.per)
                dve.wait_ge(block_done, (Idx(Z_OUT + 2 * ft.n + 1, ft.i, 2 * ft.per)).v + 1)
                dve.wait_ge(xr_loaded[ft.par], (ft.half + 1) * 16)
                res, out = tab[ft.par], at_head(x2, ft.v)
                todo = []
                for g in range(G):
                    a, b = g * GW, (g + 1) * GW
                    todo += gated_add(out[:, a:b], res[:, a:b], Z[t.par][:, g, 0:GW], G1, ft.v, a, b)
                for m, make in enumerate(todo):
                    if m == len(todo) - 1:
                        st.settle()
                        st.tell(make(), *zfree(t))
                    else:
                        st.do(make())
                dve.wait_ge(x2_squared, ft.v + 1)
                st.tell(V.tensor_tensor(ysum[:, :], ysum[:, :], res[:, :], ALU.add), x2_summed, ft.v + 1)

            with dve.Fori(0, NJ // 2) as i:
                for n in range(2):
                    out_tile(Idx(n, i, 2))
                st.restart()

            def mean_squares(bank, parts, div, fill):
                dve.wait_ge(fill_done, fill + 1)
                for n, (m, cols) in enumerate(parts):
                    ins = V.tensor_scalar(ms9[0:m, cols], bank[0:m, cols], 1.0 / div, EPS, ALU.mult, ALU.add)
                    st.do(ins) if n < len(parts) - 1 else st.tell(ins, fill_evac, fill + 1)

            def low(b, n=8):
                dve.wait_ge(w_hi_ready, b.v + 1)
                st.tell(V.tensor_tensor(w_lo[b.par][:, 0:n, :], w_raw[b.par][:, 0:n, :],
                                        w_hi[b.par][:, 0:n, :].bitcast(F32), ALU.subtract), w_split, b.v + 1)

            dve.wait_ge(w_split, B_FFN)
            low(Idx(B_FFN))
            low(Idx(B_FFN + 1))
            mean_squares(R[R_X2 % 2], ((P, slice(0, NC)), (TS, slice(NC, NC + 1))), D, R_X2)
            scales(SC2, V_FFN)
            dve.wait_ge(x2_root, 1)
            st.do(V.reciprocal(rs9[:, 0:NC], rs9[:, 0:NC]))
            st.tell(V.reciprocal(rs9[0:TS, NC:NC + 1], rs9[0:TS, NC:NC + 1]), x2_recip, 1)

            def x2_rows(n):
                fill = R_X2 + 1 + n
                t0, w = ROW_PARTS[n]
                dve.wait_ge(fill_done, fill + 1)
                st.tell(V.tensor_copy(ysum[:, t0:t0 + w], R[fill % 2][:, 0:w]), fill_evac, fill + 1)

            x2_rows(0)
            st.settle()
            for j in range(NJ):
                wait(dve, h2_ready, j - 1)
                modulate(tab[j % 2][:, 0:GW], x2[:, j, 0:GW], ysum[:, 0:GW], j, SH2, 0, GW, h2_full, j + 1)
                if j in (1, 2):
                    x2_rows(j)

            def tail_evac(g, n):
                fill = R_Y + R_Y_GRP * g + n
                if n == 0:
                    mean_squares(R[fill % 2], ((P, slice(0, 2)), (GW - 2 * P, slice(2, 3))), D, fill)
                    return
                dve.wait_ge(fill_done, fill + 1)
                if n == 1:
                    for j in range(NJ):
                        x = x2[:, j, g * GW:(g + 1) * GW]
                        ins = V.scalar_tensor_tensor(x, x, vec[:, V_FIN + j:V_FIN + j + 1], R[fill % 2][:, 0:GW],
                                                     ALU.mult, ALU.mult)
                        st.do(ins) if j < NJ - 1 else st.tell(ins, fill_evac, fill + 1)
                    return
                c, hf = (n - 2) // 2, n % 2
                m = CHUNKS[c][1]
                if hf == 0:
                    if g < G - 1:
                        wait(dve, y_staged, 16 * (len(CHUNKS) * g + c))
                    else:
                        wait(dve, y_stored[c % 2], 16 * (c // 2))
                out = ystage if g < G - 1 else tab[c % 2]
                st.tell(V.tensor_copy(out[0:m, hf * 512:(hf + 1) * 512], R[fill % 2][0:m, :]), fill_evac, fill + 1)

            def tail_recip(g):
                dve.wait_ge(y_root, g + 1)
                st.do(V.reciprocal(rs9[:, 0:2], rs9[:, 0:2]))
                st.tell(V.reciprocal(rs9[0:GW - 2 * P, 2:3], rs9[0:GW - 2 * P, 2:3]), y_recip, g + 1)

            for g in range(G):
                def in_tile(f):
                    t = Idx(T_FFN + T_GRP * g + f.n, f.i, f.per)
                    b = Idx(B_FFN + B_GRP * g + 2 * f.n, f.i, 2 * f.per)
                    count = f.v + NF * g + 1
                    sg, a = (buf[:, f.par * GW:(f.par + 1) * GW] for buf in (ta, tb))
                    low(b + 2)
                    dve.wait_ge(g_sig, count)
                    st.do(V.tensor_tensor(sg, sg, Z[t.par][:, 0, 0:GW], ALU.mult))
                    dve.wait_ge(block_done, (b + 2).v)
                    st.settle()
                    st.tell(V.tensor_tensor(a, sg, Z[t.par][:, 1, 0:GW], ALU.mult), *zfree(t))
                    low(b + 3)
                    dve.wait_ge(a_hi_ready, count)
                    st.tell(V.tensor_tensor(at_hidden(act_lo, f), a, at_hidden(act_hi, f).bitcast(F32), ALU.subtract),
                            a_ready, count)

                if g == 0:
                    dve.wait_ge(h2_ready, NJ)
                    st.settle()
                    st.do(V.memset(ysum[:, 0:GW], 0.0))
                peeled = PEELED if g else 0
                for n in range(peeled):
                    in_tile(Idx(n))
                    if n in TAIL_AT:
                        tail_evac(g - 1, TAIL_AT[n])
                    if n == 0:
                        st.do(V.memset(ysum[:, 0:GW], 0.0))
                    if n == 1:
                        tail_recip(g - 1)
                st.restart()
                with dve.Fori(peeled // 2, NF // 2) as i:
                    for n in range(2):
                        in_tile(Idx(n, i, 2))
                    st.restart()

                def ffn_out(n, i, last_pass):
                    j = Idx(n, i, 2) if i is not None else Idx(n)
                    base = B_FFN + B_GRP * g + 2 * NF
                    b = Idx(base + 3 * n, i, 6) if i is not None else Idx(base + 3 * n)
                    t = Idx(T_FFN + T_GRP * g + NF + n, i, 2) if i is not None else Idx(T_FFN + T_GRP * g + NF + n)
                    for kk in range(3):
                        if not (last_pass and 3 * n + kk + 2 >= 3 * NJ):
                            low(b + (kk + 2), OUT_K[(kk + 2) % 3])
                    dve.wait_ge(block_done, (b + 2).v + 1)
                    a, e = g * GW, (g + 1) * GW
                    x = x2[:, ds(j.v, 1), a:e].rearrange("p o t -> p (o t)")
                    todo = gated_add(x, x, Z[t.par][:, 0, 0:GW], G2, j.v, a, e)
                    for m, make in enumerate(todo):
                        if m == len(todo) - 1:
                            st.settle()
                            st.tell(make(), *zfree(t))
                        else:
                            st.do(make())
                    count = j.v + NJ * g + 1
                    dve.wait_ge(x3_squared, count)
                    st.tell(V.tensor_tensor(ysum[:, 0:GW], ysum[:, 0:GW], tb[:, n % 2 * GW:(n % 2 + 1) * GW], ALU.add),
                            x3_summed, count)

                if g < G - 1:
                    with dve.Fori(0, NJ // 2) as i:
                        for n in range(2):
                            ffn_out(n, i, False)
                        st.restart()
                else:
                    with dve.Fori(0, NJ // 2 - 1) as i:
                        for n in range(2):
                            ffn_out(n, i, False)
                        st.restart()
                    for n in range(NJ - 2, NJ):
                        ffn_out(n, None, True)

            tail_evac(G - 1, 0)
            tail_recip(G - 1)
            for n in range(1, R_Y_GRP):
                tail_evac(G - 1, n)

        @block.scalar
        def _(act):
            A = nc.scalar.activation

            def hi(b, n=8):
                act.wait_ge(*loaded(b))
                if not (b.i is None and b.n < 2):
                    act.wait_ge(block_done, (b + (-1)).v)
                A(w_hi[b.par][:, 0:n, :], w_raw[b.par][:, 0:n, :], ACT.Copy).then_inc(w_hi_ready, 1)

            def root(parts, ready):
                for n, (m, cols) in enumerate(parts):
                    last = A(rs9[0:m, cols], ms9[0:m, cols], ACT.Sqrt)
                last.then_inc(ready, 1)

            NINE = ((P, slice(0, NC)), (TS, slice(NC, NC + 1)))

            act.wait_ge(c_loaded, 32)
            A(csig[:, :], crow[:, :], ACT.Sigmoid).then_inc(csig_ready, 1)
            for t in range(NC + 1):
                m = P if t < NC else TS
                act.wait_ge(x_loaded[t % XBUF], 16 * (t // XBUF + 1))
                wait(act, x_squared, t)
                A(xsq[0:m, 0:D], xrow[t % XBUF][0:m, :], ACT.Square, accum_out=ms9[0:m, t:t + 1]).then_inc(x_squared, 1)
            act.wait_ge(lb_in, 1)
            A(lbs[:, 0, :], lbs[:, 0, :], ACT.Exp)
            A(lbs[:, 1, :], lbs[:, 1, :], ACT.Exp).then_inc(lb_exp, 1)
            act.wait_ge(ms_ready, 1)
            root(NINE, rms_root)
            hi(Idx(0))

            def shift_and_round(buf, n, m, hi_out, col, full, count, ready):
                act.wait_ge(full, count)
                bias = mod[:, col, 0:1]
                A(hi_out[:, 0:n], buf[:, 0:n], ACT.Identity, bias=bias)
                if m > n:
                    A(hi_out[:, n:m], buf[:, n:m], ACT.Copy)
                A(buf[:, 0:n], buf[:, 0:n], ACT.Identity, bias=bias).then_inc(ready, 1)

            for j in range(NJ):
                shift_and_round(hbuf[j % 3], TP, T, h_hi[:, j, :], SH1 * NJ + j, h_full, j + 1, h_hi_ready)

            def tile_read(kind, h, t, before):
                if not (t.i is None and t.n < 0):
                    act.wait_ge(block_done, t.v + 1)
                z, bias = z3(t.par), column(V_BIN + kind * NJ, h.v)
                if kind == SA:
                    wait(act, gate_ready, h.v)
                    A(g3(ta[:, :]), z, ACT.Identity, bias=bias).then_inc(zfree(t)[0], 1)
                elif kind == SB:
                    A(g3(tb[:, :]), z, ACT.Sigmoid, bias=bias).then_inc(zfree(t)[0], 1)
                elif kind == SV:
                    if before is not None:
                        act.wait_ge(fill_done, (before + N_MISC).v + 1)
                    A(g3(v[:, :]), z, ACT.Identity, bias=bias).then_inc(zfree(t)[0], 1)
                elif kind == SQ:
                    act.wait_ge(u_ready, h.v + 1)
                    A(g3(tb[:, :]), z, ACT.Sigmoid, bias=bias).then_inc(sig_ready, 1)
                elif kind == SF:
                    A(g3(ta[:, :]), z, ACT.Sigmoid, bias=bias).then_inc(zfree(t)[0], 1)
                elif kind == SOG:
                    act.wait_ge(*zfree(t + (-2)))
                    A(g3(tb[:, :]), z, ACT.Sigmoid, bias=bias).then_inc(sig_ready, 1)
                elif kind == SGA:
                    act.wait_ge(fk_ready, h.v + 1)
                    A(g3(ta[:, :]), z, ACT.Sigmoid, bias=bias).then_inc(zfree(t)[0], 1)

            def squares(fill):
                act.wait_ge(fill_evac, fill.v + 1)
                A(sqp[:, :], O[:, 0:TP], ACT.Square)
                A(sqs[:, :], O[:, TP:T], ACT.Square).then_inc(square_ready, 1)

            def rec_root(fill):
                act.wait_ge(fill_evac, fill.v + 1)
                root(NINE, root_ready)

            def body(h, t0, f, rec):
                for j in range(NT):
                    hi(t0 + (j + 1))
                    if j:
                        tile_read(ORDER[j - 1], h, t0 + (j - 1), f if rec else None)
                    elif rec:
                        tile_read(SGA, h + (-1), t0 + (-1), None)
                    if j == 5 and rec:
                        squares(f + N_OS)
                        rec_root(f + N_SS)

            heads(act, body, lambda: None)

            vq = (v, q)

            def gate_b(n):
                t = Idx(ZT + n)
                act.wait_ge(block_done, t.n + 1)
                if n == 0:
                    act.wait_ge(gate_ready, NJ)
                wait(act, gb_stored[n % 2], 16 * (n // 2))
                A(g3(tab[n % 2][:, :]), z3(t.par), ACT.Sigmoid, bias=column(V_BIN + SGB * NJ, n)) \
                    .then_inc(zfree(t)[0], 1)

            def ln_square(j):
                act.wait_ge(centred, j + 1)
                wait(act, ln_added, j - 2)
                if j == 1:
                    act.wait_ge(fill_evac, rec7(N_LV).n + 1)
                A((v, f)[j % 2][:, :] if j else ysum[:, :], yb[:, j, :], ACT.Square).then_inc(ln_squared, 1)

            def ln_apply(j):
                w, b = vec[:, V_LNW + j:V_LNW + j + 1], vec[:, V_LNB + j:V_LNB + j + 1]
                act.wait_ge(ln_scaled, j + 1)
                wait(act, ln_done, j - 1)
                A(vq[j % 2][:, :], yb[:, j, :], ACT.Sigmoid, bias=b, scale=w)
                A(yb[:, j, :], yb[:, j, :], ACT.Identity, bias=b, scale=w).then_inc(ln_affine, 1)

            def merged_hi(m):
                if m == 0:
                    act.wait_ge(operands_ready, NREADY * NJ)
                if m == 2:
                    act.wait_ge(state_stored, 16 * NJ)
                    act.wait_ge(s0_stored, 16 * NJ)
                if m < NJ:
                    act.wait_ge(m_loaded[m % MBUF], 16 * (m // MBUF + 1))
                else:
                    act.wait_ge(m_prod, m - NJ + 1)
                A(m_hi[m // NJ][:, m % NJ, :], mraw[m % MBUF][:, :], ACT.Copy).then_inc(m_hi_ready, 1)

            for j in range(NJ):
                hi(Idx(ZT + j + 1))
                if j == 0:
                    tile_read(SGA, Idx(NJ - 1), Idx(ZT - 1), None)
                else:
                    gate_b(j - 1)
                if j in (3, 4):
                    for n in range(0, 6) if j == 3 else range(6, NJ):
                        ln_square(n)
                if j == 4:
                    act.wait_ge(fill_evac, REC7 + LAST_AT[("lnss", 0)] + 1)
                    root(NINE, ln_root)
                if j == 5:
                    squares(rec7(N_OS))
                    rec_root(rec7(N_SS))
                if j == 6:
                    for n in range(4):
                        ln_apply(n)
                if j == 7:
                    merged_hi(0)
                    ln_apply(4)
                    merged_hi(1)
                    for n in range(5, NJ):
                        ln_apply(n)

            merged_hi(2)
            gate_b(NJ - 1)
            hi(Idx(Z_OUT + 1))
            for m in range(3, 2 * NJ):
                merged_hi(m)

            with act.Fori(0, NJ // 2) as i:
                for n in range(2):
                    ft = Idx(n, i, 2)
                    for kk in range(2):
                        hi(Idx(Z_OUT + 2 + 2 * n + kk, i, 4))
                    act.wait_ge(*zfree(Idx(Z_OUT + n, i, 2)))
                    A(tab[n][:, :], at_head(x2, ft.v), ACT.Square).then_inc(x2_squared, 1)
            act.wait_ge(fill_evac, R_X2 + 1)
            root(NINE, x2_root)
            for j in range(NJ):
                shift_and_round(tab[j % 2], GW, GW, h2_hi[:, j, 0:GW], SH2 * NJ + j, h2_full, j + 1, h2_hi_ready)
            act.wait_ge(h2_ready, NJ)

            def tail_root(g):
                act.wait_ge(fill_evac, R_Y + R_Y_GRP * g + 1)
                root(((P, slice(0, 2)), (GW - 2 * P, slice(2, 3))), y_root)

            for g in range(G):
                def in_tile(f):
                    t = Idx(T_FFN + T_GRP * g + f.n, f.i, f.per)
                    b = Idx(B_FFN + B_GRP * g + 2 * f.n, f.i, 2 * f.per)
                    sg, a = (buf[:, f.par * GW:(f.par + 1) * GW] for buf in (ta, tb))
                    hi(b + 2)
                    A(sg, Z[t.par][:, 0, 0:GW], ACT.Sigmoid).then_inc(g_sig, 1)
                    hi(b + 3)
                    act.wait_ge(*zfree(t))
                    A(at_hidden(act_hi, f), a, ACT.Copy).then_inc(a_hi_ready, 1)

                peeled = PEELED if g else 0
                for n in range(peeled):
                    in_tile(Idx(n))
                    if n == 0:
                        tail_root(g - 1)
                with act.Fori(peeled // 2, NF // 2) as i:
                    for n in range(2):
                        in_tile(Idx(n, i, 2))

                def ffn_out(n, i, last_pass):
                    per = 0 if i is None else 2
                    j = Idx(n, i, per)
                    b = Idx(B_FFN + B_GRP * g + 2 * NF + 3 * n, i, 3 * per)
                    t = Idx(T_FFN + T_GRP * g + NF + n, i, per)
                    for kk in range(3):
                        if not (last_pass and 3 * n + kk + 2 >= 3 * NJ):
                            hi(b + (kk + 2), OUT_K[(kk + 2) % 3])
                    act.wait_ge(*zfree(t))
                    x = x2[:, ds(j.v, 1), g * GW:(g + 1) * GW].rearrange("p o t -> p (o t)")
                    A(tb[:, n % 2 * GW:(n % 2 + 1) * GW], x, ACT.Square).then_inc(x3_squared, 1)

                with act.Fori(0, NJ // 2 - (g == G - 1)) as i:
                    for n in range(2):
                        ffn_out(n, i, False)
                if g == G - 1:
                    for n in range(NJ - 2, NJ):
                        ffn_out(n, None, True)
            tail_root(G - 1)

        @block.gpsimd
        def _(pool):
            Q = nc.gpsimd
            st = Steps(pool, gchain, met)

            def low(b):
                pool.wait_ge(w_hi_ready, b.v + 1)
                st.tell(Q.tensor_tensor(w_lo[b.par][:, :, :], w_raw[b.par][:, :, :], w_hi[b.par][:, :, :].bitcast(F32),
                                        ALU.subtract), w_split, b.v + 1)

            st.tell(Q.memset(ones[:, :], 1.0), const_ready, 1)
            st.do(Q.memset(ident[:, :], 0.0))
            st.settle()
            st.tell(Q.affine_select(out=ident[:, :], in_=ident[:, :], compare_op=ALU.not_equal, fill=1.0, base=0,
                                    pattern=[[-1, P]], channel_multiplier=1), const_ready, 2)
            low(Idx(0))
            for j in range(NJ):
                pool.wait_ge(h_hi_ready, j + 1)
                st.tell(Q.tensor_tensor(h_lo[:, j, :], hbuf[j % 3][:, 0:T], h_hi[:, j, :].bitcast(F32), ALU.subtract),
                        h_ready, j + 1)

            pool.wait_ge(h_ready, NJ)
            pool.wait_ge(adaw_used, 8)
            pool.wait_ge(x_squared, NC + 1)
            pool.wait_ge(ht_stored, 16)
            pool.wait_ge(xt_stored, 16)
            st.do(Q.memset(up[:, 0:HIST], 0.0))
            low(Idx(1))
            st.restart()

            def make_masks():
                for buf in (att[:, :, :], att_s[:, :], smask[:, :, :].bitcast(F32)):
                    st.do(Q.memset(buf, 0.0))
                for buf in (masks[:, :, :].bitcast(F32), bmask[:, :]):
                    st.do(Q.memset(buf, 1.0))

                def select(ap, op, fill, base, pattern, channel):
                    st.settle()
                    st.do(Q.affine_select(out=ap, in_=ap, compare_op=op, fill=fill, base=base, pattern=pattern,
                                          channel_multiplier=channel))

                for lv in range(LV):
                    b = 1 << lv
                    ap = masks[:, lv, :].bitcast(F32)
                    select(ap, ALU.is_ge, 0.0, 0, [[-2 * b, HB // b], [0, b]], 1)
                    select(ap, ALU.is_ge, 0.0, b - 1, [[2 * b, HB // b], [0, b]], -1)
                one = smask[:, 0, :].bitcast(F32)
                select(one, ALU.not_equal, 1.0, 0, [[-1, TS]], 1)
                one = smask[:, 1, :].bitcast(F32).rearrange("p (n two) -> p n two", two=2)[:, :, 1]
                select(one, ALU.not_equal, 1.0, 0, [[-2, TS // 2]], 1)
                one = smask[:, 2, :].bitcast(F32).rearrange("p (n four) -> p n four", four=4)[:, :, 2:4]
                st.do(Q.memset(one, 1.0))
                select(one, ALU.is_ge, 0.0, 0, [[-4, NS], [0, 2]], 1)
                select(one, ALU.is_ge, 0.0, 1, [[4, NS], [0, 2]], -1)
                select(bmask[:, :], ALU.is_ge, 0.0, 0, [[-LS, NS]], 1)
                st.settle()
                st.tell(Q.affine_select(out=bmask[:, :], in_=bmask[:, :], compare_op=ALU.is_ge, fill=0.0, base=LS - 1,
                                        pattern=[[LS, NS]], channel_multiplier=-1), masks_ready, 1)

            def gates(h, t0):
                pool.wait_ge(*zfree(t0 + (-2)))
                pool.wait_ge(*zfree(t0 + (-1)))
                wait(pool, operands_ready, NREADY * (h.v - 1))
                st.tell(Q.tensor_tensor(gate[:, :], ta[:, :], tb[:, :], ALU.mult), gate_ready, h.v)

            def channel_sum(h):
                pool.wait_ge(conv_done, h.v)
                y = at_head(yb, h.v - 1)
                if h.i is None and h.n == 1:
                    st.tell(Q.tensor_copy(ysum[:, :], y), ysum_ready, 1)
                else:
                    pool.wait_ge(ysum_ready, h.v - 1)
                    st.tell(Q.tensor_tensor(ysum[:, :], ysum[:, :], y, ALU.add), ysum_ready, h.v)

            def glu(h, t0, f, rec):
                pool.wait_ge(*zfree(t0 + 1))
                wait(pool, conv_done, h.v)
                if rec:
                    pool.wait_ge(fill_done, (f + N_MISC).v + 1)
                st.do(Q.tensor_tensor(up[:, HIST:UT], ta[:, 0:TP], tb[:, 0:TP], ALU.mult))
                st.do(Q.tensor_tensor(us[:, :, HIST:US], seqs(ta[:, TP:T]), seqs(tb[:, TP:T]), ALU.mult))
                st.do(Q.tensor_tensor(tail[:, 0:HIST], ta[:, TP - HIST:TP], tb[:, TP - HIST:TP], ALU.mult))
                st.tell(Q.tensor_tensor(tail[:, HIST:HIST + TS], ta[:, TP:T], tb[:, TP:T], ALU.mult), u_ready, h.v + 1)

            def body(h, t0, f, rec):
                for j in range(NT):
                    if rec or j:
                        low(t0 + (j + 1))
                    if j == 3 and not rec:
                        make_masks()
                    if j == 0 and rec:
                        gates(h, t0)
                    if j == 1 and rec:
                        channel_sum(h)
                    if j == 2:
                        glu(h, t0, f, rec)

            heads(pool, body, st.restart)

            for j in range(NJ):
                low(Idx(ZT + j + 1))
                if j == 0:
                    gates(Idx(NJ), Idx(ZT))
                    channel_sum(Idx(NJ))
                if j in (3, 4):
                    for n in range(1, 4) if j == 3 else range(4, NJ):
                        pool.wait_ge(ln_squared, n + 1)
                        if n > 1:
                            pool.wait_ge(ln_added, n - 1)
                        st.tell(Q.tensor_tensor(ysum[:, :], ysum[:, :], (v, f)[n % 2][:, :], ALU.add), ln_added, n)
            low(Idx(Z_OUT + 1))
            pool.wait_ge(ln_done, NJ)

            for m in range(NJ, 2 * NJ):
                pool.wait_ge(m_loaded[m % MBUF], 16 * (m // MBUF + 1))
                st.tell(Q.tensor_tensor(mraw[m % MBUF][:, :], mraw[m % MBUF][:, :], yb[:, m - NJ, :], ALU.mult),
                        m_prod, m - NJ + 1)
            for b in range(Z_OUT + 2, B_FFN):
                low(Idx(b))

            for j in range(NJ):
                pool.wait_ge(h2_hi_ready, j + 1)
                st.tell(Q.tensor_tensor(h2_lo[:, j, 0:GW], tab[j % 2][:, 0:GW], h2_hi[:, j, 0:GW].bitcast(F32),
                                        ALU.subtract), h2_ready, j + 1)
            pool.wait_ge(fill_evac, R_X2 + 1 + len(ROW_PARTS))
            for g in range(1, G):
                for j in range(NJ):
                    a, b = g * GW, (g + 1) * GW
                    n = min(b, TP) - a
                    sec = SH2 * NJ + j
                    st.settle()
                    st.do(Q.tensor_tensor(h2buf[:, :], x2[:, j, a:b], ysum[:, a:b], ALU.mult))
                    st.settle()
                    st.do(Q.tensor_scalar(h2buf[:, 0:n], h2buf[:, 0:n], am[:, j, 0:1], mod[:, sec, 0:1],
                                          ALU.mult, ALU.add))
                    if n < GW:
                        s = seqs(h2buf[:, n:GW])
                        st.do(Q.tensor_tensor(s, s, per_seq(am[:, j, 1:NSEQ]), ALU.mult))
                        st.settle()
                        st.do(Q.tensor_tensor(s, s, per_seq(mod[:, sec, 1:NSEQ]), ALU.add))
                    st.settle()
                    st.do(Q.tensor_copy(h2_hi[:, j, a:b], h2buf[:, :]))
                    st.settle()
                    st.tell(Q.tensor_tensor(h2_lo[:, j, a:b], h2buf[:, :], h2_hi[:, j, a:b].bitcast(F32),
                                            ALU.subtract), h2_ready, NJ * g + j + 1)


_INS = ("x_prompt", "x_sample", "state_hgrn", "state_conv", "c_prompt", "c_sample", "w_ada", "b_ada", "norm_mix_w",
        "w_in", "b_in", "lb_logits", "hgrn_norm_w", "conv_dw_w", "conv_dw_b", "conv_ln_w", "conv_ln_b", "w_out",
        "norm_ffn_w", "w_ffn_in", "w_ffn_out", "norm_final_w")
_OUTS = ((1, TP, D), (NS, LS, D), (1, 1, NJ, P, P), (1, 1, HIST, D), (1, NS, NJ, P, P), (1, NS, HIST, D))


def kernel(**inputs):
    import numpy as _np
    import concourse.bacc as _bacc
    from concourse.bass_utils import run_bass_kernel_spmd as _run

    nc = _bacc.Bacc("TRN2", target_bir_lowering=False, num_devices=1)
    arrays, args = {}, []
    for name in _INS:
        a = _np.ascontiguousarray(inputs[name])
        arrays[f"in_{name}_dram"] = a
        args.append(nc.dram_tensor(f"in_{name}_dram", a.shape, F32, kind="ExternalInput").ap())
    for n, shape in enumerate(_OUTS):
        args.append(nc.dram_tensor(f"out_{n}_dram", shape, F32, kind="ExternalOutput").ap())
    program(nc, *args)
    r = _run(nc, [arrays], core_ids=[0])
    return tuple(r.results[0][f"out_{n}_dram"] for n in range(len(_OUTS)))
```
